# Optimizing a Trainium2 kernel written in Bass

```python
import math
import jax
import jax.numpy as jnp
from jax import lax
import numpy as np

D_MODEL = 1024
BATCH = 1
SEQ = 256
DEPTH = 2

MEM_LEN = 256
HEAD_DIM = 128
A_HEADS = 8
B_HEADS = 8
A_WIDTH = A_HEADS * HEAD_DIM
B_WIDTH = B_HEADS * HEAD_DIM
EVEN_WIDTH = A_WIDTH + B_WIDTH
EVEN_IN = 3 * A_WIDTH + 3 * B_WIDTH + EVEN_WIDTH
C_WIDTH = D_MODEL
C_BLOCKS = 8
C_BLOCK_DIM = C_WIDTH // C_BLOCKS
CONV_WIDTH = 4
RG_C = 8.0
D_HEADS = 8
D_WIDTH = D_HEADS * HEAD_DIM
ODD_WIDTH = C_WIDTH + D_WIDTH
ODD_IN = C_WIDTH + 3 * D_WIDTH + ODD_WIDTH
HGRN_CHUNK = 32
RET_CHUNK = 64
MOBA_BLOCK = 256
MOBA_TOPK = 3
MOBA_QCHUNK = 16
ROPE_THETA = 500000.0
ROPE_DIM = HEAD_DIM // 4
RET_THETA = 10000.0
XA_HEADS = 4
XA_HEAD_DIM = 128
XA_WIDTH = XA_HEADS * XA_HEAD_DIM
N_EVEN = (DEPTH + 1) // 2
N_ODD = DEPTH // 2
EPS = 1e-6

kernel_name = 'hybrid_hgrn2_moba_rglru_retention'

def rms_norm(x, gain):
    xf = x.astype(jnp.float32)
    y = xf * lax.rsqrt(jnp.mean(xf * xf, axis=-1, keepdims=True) + EPS)
    return (y * gain.astype(jnp.float32)).astype(x.dtype)

def head_rms_norm(o, gain):
    H, d = o.shape[-2:]
    y = o * lax.rsqrt(jnp.mean(o * o, axis=-1, keepdims=True) + EPS)
    return y * gain.astype(jnp.float32).reshape(H, d)

def head_group_norm(o, gain, bias):
    H, d = o.shape[-2:]
    mu = jnp.mean(o, axis=-1, keepdims=True)
    var = jnp.mean(jnp.square(o - mu), axis=-1, keepdims=True)
    y = (o - mu) * lax.rsqrt(var + EPS)
    return y * gain.astype(jnp.float32).reshape(H, d) + bias.astype(jnp.float32).reshape(H, d)

def rotary(x, pos, rot_dim, theta):
    half = rot_dim // 2
    inv = theta ** (-jnp.arange(half, dtype=jnp.float32) / half)
    ang = pos.astype(jnp.float32)[..., None] * inv
    cos = jnp.cos(ang)[:, :, None, :]
    sin = jnp.sin(ang)[:, :, None, :]
    xf = x.astype(jnp.float32)
    x1, x2, rest = xf[..., :half], xf[..., half:rot_dim], xf[..., rot_dim:]
    out = jnp.concatenate([x1 * cos - x2 * sin, x2 * cos + x1 * sin, rest], axis=-1)
    return out.astype(x.dtype)

def chunk_state_scan(decay, u):
    def step(s, inp):
        dec, uc = inp
        return dec * s + uc, s
    s0 = jnp.zeros(u.shape[:2] + u.shape[3:], u.dtype)
    _, s_prev = lax.scan(step, s0, (jnp.moveaxis(decay, 2, 0), jnp.moveaxis(u, 2, 0)))
    return jnp.moveaxis(s_prev, 0, 2)

def hgrn2_chunked(q, f_logit, i, lb):
    B, S, H, d = q.shape
    n = S // HGRN_CHUNK
    def to_chunks(t):
        return t.astype(jnp.float32).reshape(B, n, HGRN_CHUNK, H, d).transpose(0, 3, 1, 2, 4)
    lbb = lb.astype(jnp.float32)[None, :, None, None, :]
    f = lbb + (1.0 - lbb) * jax.nn.sigmoid(to_chunks(f_logit))
    k = 1.0 - f
    qc, vc = to_chunks(q), to_chunks(i)
    b = jnp.cumsum(jnp.log(f), axis=3)
    b_last = b[:, :, :, -1:, :]
    q_dec = qc * jnp.exp(b)
    k_inv = k * jnp.exp(-b)
    k_end = k * jnp.exp(b_last - b)
    causal = jnp.tril(jnp.ones((HGRN_CHUNK, HGRN_CHUNK), bool))
    att = jnp.where(causal, jnp.einsum('bhncd,bhnsd->bhncs', q_dec, k_inv), 0.0)
    o_intra = jnp.einsum('bhncs,bhnsv->bhncv', att, vc)
    u = jnp.einsum('bhnsd,bhnsv->bhndv', k_end, vc)
    decay = jnp.exp(b_last[:, :, :, 0, :])[..., None]
    s_prev = chunk_state_scan(decay, u)
    o_inter = jnp.einsum('bhncd,bhndv->bhncv', q_dec, s_prev)
    return (o_intra + o_inter).transpose(0, 2, 3, 1, 4).reshape(B, S, H, d)

def moba_attention(q, k, v):
    B, S, H, d = q.shape
    nb = -(-S // MOBA_BLOCK)
    s_pad = nb * MOBA_BLOCK
    n_sel = min(MOBA_TOPK, nb - 1)
    n_chunks = s_pad // MOBA_QCHUNK
    scale = d ** -0.5
    def to_bhsd(t):
        t = t.astype(jnp.float32).transpose(0, 2, 1, 3)
        return jnp.pad(t, ((0, 0), (0, 0), (0, s_pad - S), (0, 0)))
    q, k, v = to_bhsd(q), to_bhsd(k), to_bhsd(v)
    k_blocks = k.reshape(B, H, nb, MOBA_BLOCK, d)
    v_blocks = v.reshape(B, H, nb, MOBA_BLOCK, d)
    if n_sel > 0:
        k_mean = jnp.mean(k_blocks, axis=3)
        gate = jnp.einsum('bhsd,bhnd->bhsn', q, k_mean)
        q_block = jnp.arange(s_pad) // MOBA_BLOCK
        fully_past = jnp.arange(nb)[None, :] < q_block[:, None]
        gate = jnp.where(fully_past, gate, -jnp.inf)
        top_val, top_idx = lax.top_k(gate, n_sel)
        sel_valid = jnp.isfinite(top_val)
    else:
        top_idx = jnp.zeros((B, H, s_pad, 0), jnp.int32)
        sel_valid = jnp.zeros((B, H, s_pad, 0), bool)
    def per_chunk(t):
        return jnp.moveaxis(t.reshape(B, H, n_chunks, MOBA_QCHUNK, *t.shape[3:]), 2, 0)
    b_ix = jnp.arange(B)[:, None, None, None]
    h_ix = jnp.arange(H)[None, :, None, None]
    n_gather = n_sel * MOBA_BLOCK
    def attend(args):
        c, qc, idx, valid = args
        start = c * MOBA_QCHUNK
        own = start // MOBA_BLOCK
        k_own = lax.dynamic_slice_in_dim(k, own * MOBA_BLOCK, MOBA_BLOCK, axis=2)
        v_own = lax.dynamic_slice_in_dim(v, own * MOBA_BLOCK, MOBA_BLOCK, axis=2)
        q_pos = start + jnp.arange(MOBA_QCHUNK)
        k_pos = own * MOBA_BLOCK + jnp.arange(MOBA_BLOCK)
        s_own = jnp.einsum('bhqd,bhjd->bhqj', qc, k_own) * scale
        s_own = jnp.where(k_pos[None, :] <= q_pos[:, None], s_own, -jnp.inf)
        k_sel = k_blocks[b_ix, h_ix, idx]
        v_sel = v_blocks[b_ix, h_ix, idx]
        s_sel = jnp.einsum('bhqd,bhqnjd->bhqnj', qc, k_sel) * scale
        s_sel = jnp.where(valid[..., None], s_sel, -jnp.inf)
        p = jax.nn.softmax(jnp.concatenate([s_sel.reshape(B, H, MOBA_QCHUNK, n_gather), s_own], axis=-1), axis=-1)
        p_sel = p[..., :n_gather].reshape(B, H, MOBA_QCHUNK, n_sel, MOBA_BLOCK)
        p_own = p[..., n_gather:]
        return jnp.einsum('bhqnj,bhqnjd->bhqd', p_sel, v_sel) + jnp.einsum('bhqj,bhjd->bhqd', p_own, v_own)
    out = lax.map(attend, (jnp.arange(n_chunks), per_chunk(q), per_chunk(top_idx), per_chunk(sel_valid)))
    out = jnp.moveaxis(out, 0, 2).reshape(B, H, s_pad, d)[:, :, :S]
    return out.transpose(0, 2, 1, 3)

def rglru_branch(cx, conv_w, conv_b, wa, ba, wx, bx, lam):
    B, S, C = cx.shape
    xc = lax.conv_general_dilated(cx, conv_w[:, None, :], window_strides=(1,),
                                  padding=[(CONV_WIDTH - 1, 0)],
                                  dimension_numbers=('NWC', 'WIO', 'NWC'),
                                  feature_group_count=C)
    xf = xc.astype(jnp.float32) + conv_b.astype(jnp.float32)
    xb = xf.reshape(B, S, C_BLOCKS, C_BLOCK_DIM)
    r = jax.nn.sigmoid(jnp.einsum('bshi,hij->bshj', xb, wa.astype(jnp.float32)).reshape(B, S, C) + ba.astype(jnp.float32))
    ig = jax.nn.sigmoid(jnp.einsum('bshi,hij->bshj', xb, wx.astype(jnp.float32)).reshape(B, S, C) + bx.astype(jnp.float32))
    log_a = -RG_C * r * jax.nn.softplus(-lam.astype(jnp.float32))
    a = jnp.exp(log_a)
    u = jnp.sqrt(-jnp.expm1(2.0 * log_a)) * ig * xf
    def combine(left, right):
        a1, b1 = left
        a2, b2 = right
        return a1 * a2, a2 * b1 + b2
    _, h = lax.associative_scan(combine, (a, u), axis=1)
    return h

def retention_chunked(q, k, v, pos):
    B, S, H, d = q.shape
    n = S // RET_CHUNK
    q = rotary(q, pos, d, RET_THETA)
    k = rotary(k, pos, d, RET_THETA)
    def to_chunks(t):
        return t.astype(jnp.float32).reshape(B, n, RET_CHUNK, H, d).transpose(0, 3, 1, 2, 4)
    qc, kc, vc = to_chunks(q), to_chunks(k) * (d ** -0.5), to_chunks(v)
    log_g = jnp.log(1.0 - 2.0 ** (-5.0 - jnp.arange(H, dtype=jnp.float32)))
    idx = jnp.arange(RET_CHUNK, dtype=jnp.float32)
    diff = idx[:, None] - idx[None, :]
    dmask = jnp.where(diff >= 0, jnp.exp(jnp.maximum(diff, 0.0) * log_g[:, None, None]), 0.0)
    att = jnp.einsum('bhncd,bhnsd->bhncs', qc, kc) * dmask[None, :, None]
    o_intra = jnp.einsum('bhncs,bhnsv->bhncv', att, vc)
    q_dec = qc * jnp.exp((idx + 1.0)[None, :] * log_g[:, None])[None, :, None, :, None]
    k_end = kc * jnp.exp((RET_CHUNK - 1.0 - idx)[None, :] * log_g[:, None])[None, :, None, :, None]
    u = jnp.einsum('bhnsd,bhnsv->bhndv', k_end, vc)
    chunk_decay = jnp.broadcast_to(jnp.exp(RET_CHUNK * log_g)[None, :, None, None, None], (1, H, n, 1, 1))
    s_prev = chunk_state_scan(chunk_decay, u)
    o_inter = jnp.einsum('bhncd,bhndv->bhncv', q_dec, s_prev)
    return (o_intra + o_inter).transpose(0, 2, 3, 1, 4).reshape(B, S, H, d)

def even_mixer(xn, pos, lb, w_in, hgrn_gain, w_out):
    B, S, _ = xn.shape
    h = jnp.einsum('bsd,de->bse', xn, w_in)
    splits = np.cumsum([A_WIDTH] * 3 + [B_WIDTH] * 3).tolist()
    aq, af, ai, bq, bk, bv, z = jnp.split(h, splits, axis=-1)
    def heads(t):
        return t.reshape(B, S, -1, HEAD_DIM)
    oa = hgrn2_chunked(heads(aq), heads(af), heads(ai), lb.reshape(A_HEADS, HEAD_DIM))
    oa = head_rms_norm(oa, hgrn_gain)
    ob = moba_attention(rotary(heads(bq), pos, ROPE_DIM, ROPE_THETA),
                        rotary(heads(bk), pos, ROPE_DIM, ROPE_THETA), heads(bv))
    y = jnp.concatenate([oa.reshape(B, S, A_WIDTH), ob.reshape(B, S, B_WIDTH)], axis=-1).astype(xn.dtype)
    y = y * jax.nn.silu(z)
    return jnp.einsum('bse,ed->bsd', y, w_out)

def odd_mixer(xn, pos, w_in, conv_w, conv_b, wa, ba, wx, bx, lam, ret_gain, ret_bias, w_out):
    B, S, _ = xn.shape
    h = jnp.einsum('bsd,de->bse', xn, w_in)
    splits = np.cumsum([C_WIDTH] + [D_WIDTH] * 3).tolist()
    cx, dq, dk, dv, z = jnp.split(h, splits, axis=-1)
    oc = rglru_branch(cx, conv_w, conv_b, wa, ba, wx, bx, lam)
    def heads(t):
        return t.reshape(B, S, D_HEADS, HEAD_DIM)
    od = head_group_norm(retention_chunked(heads(dq), heads(dk), heads(dv), pos), ret_gain, ret_bias)
    y = jnp.concatenate([oc, od.reshape(B, S, D_WIDTH)], axis=-1).astype(xn.dtype)
    y = y * jax.nn.silu(z)
    return jnp.einsum('bse,ed->bsd', y, w_out)

def memory_cross_attention(xn, mem, mem_gain, wq, wkv, wo):
    B, S, _ = xn.shape
    M = mem.shape[1]
    mn = rms_norm(mem, mem_gain)
    q = jnp.einsum('bsd,de->bse', xn, wq).reshape(B, S, XA_HEADS, XA_HEAD_DIM)
    kv = jnp.einsum('bmd,de->bme', mn, wkv)
    k, v = jnp.split(kv, 2, axis=-1)
    k = k.reshape(B, M, XA_HEADS, XA_HEAD_DIM)
    v = v.reshape(B, M, XA_HEADS, XA_HEAD_DIM)
    s = jnp.einsum('bqhd,bkhd->bhqk', q.astype(jnp.float32), k.astype(jnp.float32)) * (XA_HEAD_DIM ** -0.5)
    p = jax.nn.softmax(s, axis=-1)
    o = jnp.einsum('bhqk,bkhd->bqhd', p, v.astype(jnp.float32)).reshape(B, S, XA_WIDTH).astype(xn.dtype)
    return jnp.einsum('bse,ed->bsd', o, wo)

def setup_inputs(seed: int = 0) -> dict:
    key = jax.random.key(seed)
    ks = jax.random.split(key, 26)
    def w(k, shape, fan_in, scale=1.0):
        return jax.random.normal(k, shape, jnp.float32) * (scale * fan_in ** -0.5)
    def gain(k, shape):
        return 1.0 + 0.02 * jax.random.normal(k, shape, jnp.float32)
    def small(k, shape):
        return 0.02 * jax.random.normal(k, shape, jnp.float32)
    x = jax.random.normal(ks[0], (BATCH, SEQ, D_MODEL), jnp.float32)
    mem = jax.random.normal(ks[1], (BATCH, MEM_LEN, D_MODEL), jnp.float32)
    offsets = jax.random.randint(ks[2], (BATCH, 1), 0, 4096, dtype=jnp.int32)
    positions = (jnp.arange(SEQ, dtype=jnp.int32)[None, :] + offsets).astype(jnp.int32)
    u = jax.random.uniform(ks[16], (N_ODD, C_WIDTH), jnp.float32, minval=0.9, maxval=0.999)
    a0 = u ** (1.0 / RG_C)
    lam = jnp.log(a0) - jnp.log1p(-a0)
    return {
        'x': x,
        'mem': mem,
        'positions': positions,
        'hgrn_lb_logits': 0.5 * jax.random.normal(ks[3], (DEPTH + 1, A_WIDTH), jnp.float32),
        'ev_norm': gain(ks[4], (N_EVEN, D_MODEL)),
        'ev_w_in': w(ks[5], (N_EVEN, D_MODEL, EVEN_IN), D_MODEL),
        'ev_hgrn_gain': gain(ks[6], (N_EVEN, A_WIDTH)),
        'ev_w_out': w(ks[7], (N_EVEN, EVEN_WIDTH, D_MODEL), EVEN_WIDTH),
        'od_norm': gain(ks[8], (N_ODD, D_MODEL)),
        'od_w_in': w(ks[9], (N_ODD, D_MODEL, ODD_IN), D_MODEL),
        'od_conv_w': w(ks[10], (N_ODD, CONV_WIDTH, C_WIDTH), CONV_WIDTH),
        'od_conv_b': small(ks[11], (N_ODD, C_WIDTH)),
        'od_rg_wa': w(ks[12], (N_ODD, C_BLOCKS, C_BLOCK_DIM, C_BLOCK_DIM), C_BLOCK_DIM),
        'od_rg_ba': small(ks[13], (N_ODD, C_WIDTH)),
        'od_rg_wx': w(ks[14], (N_ODD, C_BLOCKS, C_BLOCK_DIM, C_BLOCK_DIM), C_BLOCK_DIM),
        'od_rg_bx': small(ks[15], (N_ODD, C_WIDTH)),
        'od_rg_lambda': lam,
        'od_ret_gain': gain(ks[17], (N_ODD, D_WIDTH)),
        'od_ret_bias': small(ks[18], (N_ODD, D_WIDTH)),
        'od_w_out': w(ks[19], (N_ODD, ODD_WIDTH, D_MODEL), ODD_WIDTH),
        'xa_norm': gain(ks[20], (DEPTH, D_MODEL)),
        'xa_mem_norm': gain(ks[21], (DEPTH, D_MODEL)),
        'xa_wq': w(ks[22], (DEPTH, D_MODEL, XA_WIDTH), D_MODEL),
        'xa_wkv': w(ks[23], (DEPTH, D_MODEL, 2 * XA_WIDTH), D_MODEL),
        'xa_wo': w(ks[24], (DEPTH, XA_WIDTH, D_MODEL), XA_WIDTH),
        'final_norm': gain(ks[25], (D_MODEL,)),
    }

def reference(x, mem, positions, hgrn_lb_logits, ev_norm, ev_w_in, ev_hgrn_gain, ev_w_out,
              od_norm, od_w_in, od_conv_w, od_conv_b, od_rg_wa, od_rg_ba, od_rg_wx, od_rg_bx,
              od_rg_lambda, od_ret_gain, od_ret_bias, od_w_out,
              xa_norm, xa_mem_norm, xa_wq, xa_wkv, xa_wo, final_norm):
    lb_all = jnp.cumsum(jax.nn.softmax(hgrn_lb_logits.astype(jnp.float32), axis=0), axis=0)
    for layer in range(DEPTH):
        if layer % 2 == 0:
            e = layer // 2
            x = x + even_mixer(rms_norm(x, ev_norm[e]), positions, lb_all[layer],
                               ev_w_in[e], ev_hgrn_gain[e], ev_w_out[e])
        else:
            o = layer // 2
            x = x + odd_mixer(rms_norm(x, od_norm[o]), positions, od_w_in[o], od_conv_w[o], od_conv_b[o],
                              od_rg_wa[o], od_rg_ba[o], od_rg_wx[o], od_rg_bx[o], od_rg_lambda[o],
                              od_ret_gain[o], od_ret_bias[o], od_w_out[o])
        x = x + memory_cross_attention(rms_norm(x, xa_norm[layer]), mem, xa_mem_norm[layer],
                                       xa_wq[layer], xa_wkv[layer], xa_wo[layer])
    return rms_norm(x, final_norm)


_drawn_inputs = setup_inputs


def setup_inputs(seed=0):
    import zlib

    import numpy as np

    out = dict(_drawn_inputs(seed))
    spreads = {}
    factors = {'ev_hgrn_gain': 5.115,
     'od_norm': 3.588,
     'od_rg_ba': 22.831,
     'od_rg_bx': 8.0,
     'od_ret_gain': 8.0,
     'od_ret_bias': 8.0,
     'xa_norm': 8.0,
     'xa_mem_norm': 8.0,
     'final_norm': 7.824}
    for name, (base, spread) in spreads.items():
        noise = np.random.default_rng([zlib.crc32(name.encode()), seed]).standard_normal(out[name].shape)
        drawn = base * np.exp(spread * noise) if base else spread * noise
        out[name] = jnp.asarray(drawn.astype(out[name].dtype))
    for name, factor in factors.items():
        out[name] = (out[name] * factor).astype(out[name].dtype)
    return out
```

```python
from contextlib import ExitStack

import numpy as np

import concourse.bass as bass
from concourse import mybir

F32 = mybir.dt.float32
F32R = mybir.dt.float32r
I32 = mybir.dt.int32
ALU = mybir.AluOpType
ACT = mybir.ActivationFunctionType
AX_X = mybir.AxisListType.X

P = 128
S = 256
D = 1024
KC = D // P
T = S // P
HG = 4
EPS = 1e-6
HGRN_CHUNK = 32
NCH = S // HGRN_CHUNK
RG_C = 8.0
SCALE = float(P) ** -0.5
NEG = -1e30
FAR = 1e6
ROUND = 1.5 * 2.0 ** 23
TWO_PI_A = 6.28125
TWO_PI_B = float(np.float32(round((2 * np.pi - TWO_PI_A) * 2.0 ** 20) / 2.0 ** 20))
TWO_PI_C = float(2 * np.pi - TWO_PI_A - TWO_PI_B)
PI_IN = 3.1415925

PARAM_ROWS = [("ev_norm", 8), ("hgrn_lb_logits", 24), ("ev_hgrn_gain", 8), ("od_norm", 8), ("od_conv_w", 32),
              ("od_conv_b", 8), ("od_rg_ba", 8), ("od_rg_bx", 8), ("od_rg_lambda", 8), ("od_ret_gain", 8),
              ("od_ret_bias", 8), ("xa_norm", 16), ("xa_mem_norm", 16)]
PARAM_AT, N_ROWS = {}, 0
for _name, _rows in PARAM_ROWS:
    PARAM_AT[_name] = N_ROWS
    N_ROWS += _rows

C_INV_RET, C_INV_MOBA, C_SIGN_RET, C_SIGN_MOBA, C_LOG_G, N_CONST = 0, 1, 2, 3, 4, 12

SLABS = []
for _g in range(2):
    SLABS += [("A", "f", "F", _g), ("A", "q", "F", _g), ("A", "i", "T", _g), ("A", "z", "F", _g)]
for _g in range(2):
    SLABS += [("B", "q", "F", _g), ("B", "k", "F", _g), ("B", "v", "T", _g), ("B", "z", "F", _g)]
SLABS += [("OUT0", (0, 0), "T", 0), ("OUT0", (1, 0), "T", 0), ("OUT0", (1, 1), "T", 0), ("OUT0", (0, 1), "T", 0)]
SLABS += [("XA0", "k", "F", 0), ("XA0", "q", "F", 0), ("XA0", "v", "T", 0), ("XA0", "o", "W", 0), ("XA1", "k", "F", 0)]
for _g in range(2):
    SLABS += [("C", "x", "F", _g), ("C", "z", "F", _g)]
for _g in range(2):
    SLABS += [("D", "q", "F", _g), ("D", "k", "F", _g), ("D", "v", "T", _g), ("D", "z", "F", _g)]
SLABS += [("OUT1", (0, 0), "T", 0), ("OUT1", (1, 0), "T", 0), ("OUT1", (1, 1), "T", 0), ("OUT1", (0, 1), "T", 0)]
SLABS += [("XA1", "v", "T", 0), ("XA1", "q", "F", 0), ("XA1", "o", "W", 0)]
NSLAB = len(SLABS)


def slab(stage, part, g=0):
    return [n for n, s in enumerate(SLABS) if s[0] == stage and s[1] == part and s[3] == g][0]


TURN = {}
_t = 0
for _n, _s in enumerate(SLABS):
    if _s[0] in ("OUT0", "OUT1"):
        if _s[1] in ((0, 0), (1, 1)):
            TURN[_n] = _t
            _t += 1
        else:
            TURN[_n] = _t - 1
    elif _s[2] == "W":
        TURN[_n] = _t
        _t += 2
    else:
        TURN[_n] = _t
        _t += 1


def hybrid_trunk(nc, I, out):
    with ExitStack() as ctx:
        def sb(name, shape, dt=F32):
            return ctx.enter_context(nc.sbuf_tensor(name, shape, dt))

        def sem(name):
            return ctx.enter_context(nc.semaphore(name))

        raw = sb("raw_weights", [P, 2, 4096])
        w_hi = sb("w_hi", [P, 4, 1024], F32R)
        w_lo = sb("w_lo", [P, 4, 1024], F32R)
        xT_hi = sb("xT_hi", [P, KC, S], F32R)
        xT_lo = sb("xT_lo", [P, KC, S], F32R)
        y_hi = sb("y_hi", [P, 2 * KC, S], F32R)
        y_lo = sb("y_lo", [P, 2 * KC, S], F32R)
        x_sb = sb("x_residual", [P, T, D])
        memT = sb("memT", [P, KC, S])
        W = sb("work", [P, 6, 1024])
        v_sb = sb("v_rows", [P, T, 512])
        zs = sb("z_silu", [P, 4, S])
        att = sb("att", [P, 4, S])
        kend_rows = sb("kend_rows", [P, T, 4, P])
        states = sb("states", [P, 4, NCH - 1, P])
        kx = sb("mem_keys", [P, 4, S])
        prm_rows = sb("prm_rows", [P, 2, P])
        prm = sb("prm", [P, N_ROWS])
        const = sb("const", [P, N_CONST])
        ident = sb("ident", [P, P])
        avg = sb("avg", [P, P])
        center = sb("center", [P, P])
        causal = sb("causal", [P, 3 * P])
        chunk_mask_f = sb("chunk_mask_f", [P, P])
        chunk_mask = sb("chunk_mask", [P, P], I32)
        scan_mask = sb("scan_mask", [P, 1024])
        dist = sb("dist", [P, 3 * P])
        dmask = sb("dmask", [P, 2, 3 * P])
        trig = sb("trig", [P, 4, S])
        lbp = sb("lbp", [P, 6, KC])
        soft = sb("soft", [P, 8, KC])
        st = sb("stats", [P, 64])
        rg_w = states[:, :, :, :].rearrange("p a b c -> p (a b c)")[:, 0:2048].rearrange(
            "p (m h c) -> p m h c", m=4, h=4)
        fgain = kend_rows[:, :, :, :].rearrange("p a b c -> p (a b c)")

        proj = [ctx.enter_context(nc.psum_tensor(f"proj{i}", [P, 512], F32)) for i in range(4)]
        head = [ctx.enter_context(nc.psum_tensor(f"head{i}", [P, 512], F32)) for i in range(4)]

        w_landed = [sem(f"w_landed{i}") for i in range(2)]
        hi_ready = sem("hi_ready")
        lo_ready = sem("lo_ready")
        quarter_used = sem("quarter_used")
        bank_free = [sem(f"bank_free{i}") for i in range(4)]
        x_landed = sem("x_landed")
        mem_landed = sem("mem_landed")
        prm_landed = sem("prm_landed")
        pos_landed = sem("pos_landed")
        rg_landed = [sem(f"rg_landed{g}") for g in range(2)]
        fgain_landed = sem("fgain_landed")
        out_landed = sem("out_landed")
        masks_ready = sem("masks_ready")
        prm_turned = sem("prm_turned")
        prm_ready = sem("prm_ready")
        lb_max = sem("lb_max")
        lb_exp = sem("lb_exp")
        soft_abs = sem("soft_abs")
        soft_exp = sem("soft_exp")
        soft_ready = sem("soft_ready")
        angles_ready = sem("angles_ready")
        trig_ready = sem("trig_ready")
        trig_signed = sem("trig_signed")
        sumsq = sem("sumsq")
        inv_ready = sem("inv_ready")
        rstd_ready = sem("rstd_ready")
        normed = sem("normed")
        turned = sem("turned")
        memT_ready = sem("memT_ready")
        xT_hi_ready = sem("xT_hi_ready")
        xT_lo_ready = sem("xT_lo_ready")
        mn_hi_ready = sem("mn_hi_ready")
        mn_lo_ready = sem("mn_lo_ready")
        x_added = sem("x_added")
        z_ready = sem("z_ready")
        v_ready = sem("v_ready")
        y_ready = sem("y_ready")
        y_hi_ready = sem("y_hi_ready")
        y_lo_ready = sem("y_lo_ready")
        f_sig = sem("f_sig")
        f_ready = sem("f_ready")
        lnf_ready = sem("lnf_ready")
        b_ready = sem("b_ready")
        exps_ready = sem("exps_ready")
        bend_ready = sem("bend_ready")
        eend_ready = sem("eend_ready")
        qdec_ready = sem("qdec_ready")
        kinv_ready = sem("kinv_ready")
        kend_ready = sem("kend_ready")
        att_psum = sem("att_psum")
        att_ready = sem("att_ready")
        kend_turned = sem("kend_turned")
        kend_rows_ready = sem("kend_rows_ready")
        u_psum = sem("u_psum")
        state_ready = sem("state_ready")
        o_psum = sem("o_psum")
        o_square = sem("o_square")
        ms_psum = sem("ms_psum")
        o_rstd = sem("o_rstd")
        q_rows = sem("q_copied")
        k_rows = sem("k_copied")
        q_ready = sem("q_ready")
        k_ready = sem("k_ready")
        scores = sem("scores")
        row_max = sem("row_max")
        probs = sem("probs")
        probs_norm = sem("probs_norm")
        probs_turned = sem("probs_turned")
        probsT_ready = sem("probsT_ready")
        cx_ready = sem("cx_ready")
        xf_ready = sem("xf_ready")
        gates_psum = sem("gates_psum")
        rgate_ready = sem("rgate_ready")
        igate_ready = sem("igate_ready")
        decay_ready = sem("decay_ready")
        one_minus = sem("one_minus")
        root_ready = sem("root_ready")
        h_ready = sem("h_ready")
        dmask_ready = sem("dmask_ready")
        o_copied = sem("o_copied")
        cen_psum = sem("cen_psum")
        fin_ready = sem("fin_ready")

        def wview(i, n=1):
            return W[:, i:i + n, :].rearrange("p a b -> p (a b)")

        def blocks(i):
            return W[:, i, :].rearrange("p (h t) -> p h t", h=4)

        def param(name, k):
            c = PARAM_AT[name] + k
            return prm[:, c:c + 1]

        def dram_slab(n):
            stage, part, kind, g = SLABS[n]
            if stage in ("A", "B"):
                col = {"A": "qfi", "B": "qkv"}[stage].find(part) * D + 3 * D * (stage == "B")
                if part == "z":
                    col = 6 * D + D * (stage == "B")
                return I["ev_w_in"][0][:, col + 512 * g:col + 512 * g + 512].rearrange("(k p) n -> p k n", p=P)
            if stage in ("C", "D"):
                col = {"x": 0, "q": D, "k": 2 * D, "v": 3 * D, "z": 4 * D + D * (stage == "D")}[part]
                return I["od_w_in"][0][:, col + 512 * g:col + 512 * g + 512].rearrange("(k p) n -> p k n", p=P)
            if stage in ("OUT0", "OUT1"):
                w = I["ev_w_out" if stage == "OUT0" else "od_w_out"][0]
                kh, c = part
                return w[D * kh:D * kh + D, 512 * c:512 * c + 512].rearrange("(k p) n -> p k n", p=P)
            layer = int(stage[2])
            if part == "q":
                return I["xa_wq"][layer].rearrange("(k p) n -> p k n", p=P)
            if part in "kv":
                c = 512 * (part == "v")
                return I["xa_wkv"][layer][:, c:c + 512].rearrange("(k p) n -> p k n", p=P)
            return I["xa_wo"][layer].rearrange("(k p) n -> p k n", p=P)

        def raw_quarter(n, q):
            kind = SLABS[n][2]
            r = raw[:, n % 2, :]
            if kind == "F":
                return r.rearrange("p (k c) -> p k c", k=KC)[:, :, P * q:P * q + P]
            if kind == "T":
                return r.rearrange("p (k c) -> p k c", k=KC)[:, 2 * q:2 * q + 2, :]
            return r.rearrange("p (k c) -> p k c", k=4)[:, 2 * (q % 2):2 * (q % 2) + 2,
                                                        512 * (q // 2):512 * (q // 2) + 512]

        def ring_quarter(ring, n, q):
            return ring[:, q, :].rearrange("p (k c) -> p k c", k=KC if SLABS[n][2] == "F" else 2)

        def bank(n, u, half=0):
            return proj[2 * ((TURN[n] + half) % 2) + u]

        def free_of(n, u, half=0):
            return bank_free[2 * ((TURN[n] + half) % 2) + u]

        def filled(eng, n, u, half=0):
            kind = SLABS[n][2]
            eng.wait_ge(quarter_used, 4 * n + (2 * u + 2 if kind == "F" else 2 * half + 2 if kind == "W" else 4))

        def y_src(i):
            return blocks({0: 0, 1: 0, 2: 0, 3: 0, 4: 1, 5: 1, 6: 1, 7: 1}[i])

        block = ctx.enter_context(nc.Block())

        @block.sync
        def _(sp):
            sp.dma_start(x_sb[:], I["x"][0].rearrange("(t p) d -> p t d", p=P)).then_inc(x_landed, 16)
            for n in range(NSLAB):
                if n == slab("C", "x", 0):
                    for m, name in enumerate(("od_rg_wa", "od_rg_wx")):
                        for g in range(2):
                            sp.dma_start(rg_w[:, 2 * g + m], I[name][0][4 * g:4 * g + 4].rearrange(
                                "h i j -> i h j")).then_inc(rg_landed[g], 16)
                    sp.dma_start(fgain, I["final_norm"].rearrange("(a d) -> a d", a=1).broadcast_to([P, D])
                                 ).then_inc(fgain_landed, 16)
                if n >= 2:
                    sp.wait_ge(lo_ready, 4 * (n - 1))
                sp.dma_start(raw[:, n % 2, :].rearrange("p (k c) -> p k c", k=4 if SLABS[n][2] == "W" else KC),
                             dram_slab(n)).then_inc(w_landed[n % 2], 16)
            sp.wait_ge(fin_ready, T)
            sp.dma_start(out[0].rearrange("(t p) d -> p t d", p=P), x_sb[:]).then_inc(out_landed, 16)
            sp.wait_ge(out_landed, 16)

        @block.gpsimd
        def _(pool):
            pool.memset(ident[:], 0.0)
            pool.memset(avg[:], 1.0 / P)
            pool.memset(center[:], -1.0 / P)
            pool.memset(causal[:], 0.0)
            pool.memset(chunk_mask_f[:], 1.0)
            pool.memset(scan_mask[:], 1.0)
            pool.iota(dist[:, 0:S], pattern=[[1, S]], base=0, channel_multiplier=-1,
                      allow_small_or_imprecise_dtypes=True)
            pool.iota(dist[:, S:3 * P], pattern=[[1, P]], base=0, channel_multiplier=-1,
                      allow_small_or_imprecise_dtypes=True)
            pool.drain()
            pool.affine_select(out=ident[:], in_=ident[:], compare_op=ALU.not_equal, fill=1.0, base=0,
                               pattern=[[-1, P]], channel_multiplier=1).then_inc(masks_ready, 1)
            pool.affine_select(out=center[:], in_=center[:], compare_op=ALU.not_equal, fill=1.0 - 1.0 / P, base=0,
                               pattern=[[-1, P]], channel_multiplier=1)
            for c in (0, 2 * P):
                pool.affine_select(out=causal[:, c:c + P], in_=causal[:, c:c + P], compare_op=ALU.is_ge, fill=NEG,
                                   base=0, pattern=[[-1, P]], channel_multiplier=1)
            pool.affine_select(out=chunk_mask_f[:], in_=chunk_mask_f[:], compare_op=ALU.is_ge, fill=0.0, base=0,
                               pattern=[[1, P]], channel_multiplier=-1)
            pool.drain()
            pool.affine_select(out=chunk_mask_f[:], in_=chunk_mask_f[:], compare_op=ALU.is_ge, fill=0.0, base=0,
                               pattern=[[-HGRN_CHUNK, P // HGRN_CHUNK], [0, HGRN_CHUNK]], channel_multiplier=1)
            pool.affine_select(out=dist[:, 0:S], in_=dist[:, 0:S], compare_op=ALU.is_ge, fill=FAR, base=0,
                               pattern=[[1, S]], channel_multiplier=-1)
            pool.affine_select(out=dist[:, S:3 * P], in_=dist[:, S:3 * P], compare_op=ALU.is_ge, fill=FAR, base=0,
                               pattern=[[1, P]], channel_multiplier=-1)
            pool.memset(scan_mask[:].rearrange("p (c s) -> p c s", s=HGRN_CHUNK)[:, :, 0:1], 0.0)
            pool.memset(att[:], 0.0)
            pool.drain()
            pool.tensor_copy(chunk_mask[:], chunk_mask_f[:]).then_inc(masks_ready, 1)

            for i, G in enumerate((0, 1, 2, 3, 0, 1, 2, 3)):
                pool.wait_ge(y_hi_ready, i + 1 + 2 * (i >= 4))
                pool.tensor_tensor(y_lo[:, 4 * G:4 * G + 4, :], y_src(i), y_hi[:, 4 * G:4 * G + 4, :].bitcast(F32),
                                   ALU.subtract).then_inc(y_lo_ready, 1)

        @block.scalar
        def _(act):
            act.dma_start(W[:, 2:4, :], I["mem"][0].rearrange("(t p) d -> p t d", p=P)).then_inc(mem_landed, 16)
            act.dma_start(const[:], I["shape_constants"]).then_inc(pos_landed, 16)
            act.dma_start(W[:, 5, 0:S].bitcast(I32), I["positions"].broadcast_to([P, S])).then_inc(pos_landed, 16)
            for name, rows in PARAM_ROWS:
                src = I[name]
                src = (src.rearrange("(k p) -> k p", p=P) if len(src.shape) == 1 else
                       src.rearrange("a (k p) -> (a k) p", p=P) if len(src.shape) == 2 else
                       src.rearrange("a b (k p) -> (a b k) p", p=P))
                r = PARAM_AT[name]
                t = r // P
                act.dma_start(prm_rows[r - P * t:r - P * t + rows, t, :], src).then_inc(prm_landed, 16)

            def hi(n, q):
                if q == 0:
                    act.wait_ge(w_landed[n % 2], 16 * (n // 2 + 1))
                if n >= 1:
                    act.wait_ge(quarter_used, 4 * (n - 1) + q + 1)
                act.activation(ring_quarter(w_hi, n, q), raw_quarter(n, q), ACT.Copy).then_inc(hi_ready, 1)

            def his(n, qs):
                if n < NSLAB:
                    for q in qs:
                        hi(n, q)

            def square_sums(src, junk):
                for t in range(T):
                    act.drain()
                    act.activation(junk, src[:, t, :], ACT.Square, accum_out=st[:, t:t + 1]).then_inc(sumsq, 1)

            def root(i):
                act.wait_ge(inv_ready, i + 1)
                act.activation(st[:, 4:6], st[:, 2:4], ACT.Sqrt).then_inc(rstd_ready, 1)

            def xT_high(i, gain, gk):
                for k in range(KC):
                    if k % 2 == 0:
                        act.wait_ge(turned, 4 * (i + 1) + k // 2 + 1)
                    act.activation(xT_hi[:, k, :], head[k // 2][:, S * (k % 2):S * (k % 2) + S], ACT.Copy,
                                   scale=param(gain, gk + k)).then_inc(xT_hi_ready, 1)

            def mn_high(layer, use):
                for k in range(KC):
                    act.activation(y_hi[:, KC + k, :], memT[:, k, :], ACT.Copy,
                                   scale=param("xa_mem_norm", KC * layer + k)).then_inc(mn_hi_ready, 1)

            def silu(n, u):
                filled(act, n, u)
                i = {"A": 0, "B": 2, "C": 4, "D": 6}[SLABS[n][0]] + SLABS[n][3]
                if i:
                    act.wait_ge(y_ready, i)
                act.activation(zs[:, 2 * u:2 * u + 2, :], bank(n, u)[:].rearrange("p (h t) -> p h t", h=2), ACT.Silu
                               ).then_inc(z_ready, 1)

            def silu_free(n, u):
                silu(n, u)
                act.drain().then_inc(free_of(n, u), 1)

            def copy_bank(n, u, dst, s):
                filled(act, n, u)
                act.activation(dst, bank(n, u)[:], ACT.Copy).then_inc(s, 1)
                act.drain().then_inc(free_of(n, u), 1)

            def v_rows(n):
                for t in range(T):
                    copy_bank(n, t, v_sb[:, t, :], v_ready)

            def y_high(i, G):
                act.wait_ge(y_ready, i + 1)
                act.activation(y_hi[:, 4 * G:4 * G + 4, :], y_src(i), ACT.Copy).then_inc(y_hi_ready, 1)

            act.wait_ge(mem_landed, 16)
            square_sums(W[:, 2:4, :], wview(4))
            root(0)
            act.wait_ge(x_landed, 16)
            act.wait_ge(normed, 1)
            square_sums(x_sb, wview(4))
            root(1)
            act.wait_ge(prm_turned, 1)
            act.activation(prm[:, 0:P], proj[0][:, 0:P], ACT.Copy)
            act.activation(prm[:, P:N_ROWS], proj[0][:, P:N_ROWS], ACT.Copy).then_inc(prm_ready, 1)
            for j in range(4):
                act.wait_ge(turned, j + 1)
                act.activation(memT[:, 2 * j:2 * j + 2, :], head[j][:].rearrange("p (k t) -> p k t", k=2), ACT.Copy
                               ).then_inc(memT_ready, 1)
            act.drain()
            his(0, range(2))
            xT_high(0, "ev_norm", 0)
            his(0, range(2, 4))
            act.wait_ge(lb_max, 1)
            act.activation(lbp[:, 0:3, :], lbp[:, 0:3, :], ACT.Exp).then_inc(lb_exp, 1)
            act.wait_ge(soft_abs, 1)
            act.activation(soft[:, 2, :], soft[:, 1, :], ACT.Exp, scale=-1.0).then_inc(soft_exp, 1)
            act.wait_ge(angles_ready, 1)
            act.activation(trig[:], trig[:], ACT.Sin).then_inc(trig_ready, 1)

            def stage_a(g):
                f, q, i, z = (slab("A", c, g) for c in "fqiz")
                if g:
                    act.wait_ge(y_lo_ready, g)
                his(f + 1, [0])
                filled(act, f, 0)
                act.activation(W[:, 0, 0:512], bank(f, 0)[:], ACT.Sigmoid).then_inc(f_sig, 1)
                act.drain().then_inc(free_of(f, 0), 1)
                his(f + 1, [1, 2])
                filled(act, f, 1)
                act.activation(W[:, 0, 512:1024], bank(f, 1)[:], ACT.Sigmoid).then_inc(f_sig, 1)
                act.drain().then_inc(free_of(f, 1), 1)
                his(f + 1, [3])
                act.wait_ge(f_ready, g + 1)
                act.activation(wview(0), wview(0), ACT.Ln).then_inc(lnf_ready, 1)
                his(f + 2, [0])
                act.wait_ge(b_ready, g + 1)
                act.activation(wview(3), wview(2), ACT.Exp).then_inc(exps_ready, 1)
                act.activation(wview(0), wview(2), ACT.Exp, scale=-1.0).then_inc(exps_ready, 1)
                his(f + 2, [1])
                act.wait_ge(bend_ready, g + 1)
                act.activation(wview(5), wview(5), ACT.Exp).then_inc(eend_ready, 1)
                his(f + 2, [2, 3])
                his(f + 3, [0, 1])
                for u in range(2):
                    act.wait_ge(kend_turned, 2 * g + u + 1)
                    act.activation(kend_rows[:, u, :, :].rearrange("p h d -> p (h d)"), head[2 + u][:], ACT.Copy
                                   ).then_inc(kend_rows_ready, 1)
                his(f + 3, [2, 3])
                v_rows(i)
                his(f + 4, [0])
                his(f + 4, [1])
                silu_free(z, 0)
                his(f + 4, [2])
                his(f + 4, [3])
                silu_free(z, 1)
                for u in range(2):
                    act.wait_ge(o_psum, 2 * g + u + 1)
                    act.activation(W[:, 1, 512 * u:512 * u + 512], head[u][:], ACT.Square).then_inc(o_square, 1)
                for u in range(2):
                    act.wait_ge(ms_psum, 2 * g + u + 1)
                    act.activation(W[:, 5, 512 * u:512 * u + 512], head[2 + u][:], ACT.Ln, bias=st[:, 60:61])
                act.drain()
                act.activation(wview(5), wview(5), ACT.Exp, scale=-0.5).then_inc(o_rstd, 1)
                y_high(g, g)

            def softmax_exp(i, h, moba, cnt):
                act.wait_ge(row_max, i)
                for t in range(T):
                    if moba:
                        pr = wview(2, 2)[:, 384 * h + 128 * t:384 * h + 128 + 256 * t]
                    else:
                        pr = wview(2, 2)[:, 512 * h + 256 * t:512 * h + 256 * t + 256]
                    c = 2 * h + t
                    src = pr if moba else head[h][:, 256 * t:256 * t + 256]
                    act.activation(pr, src, ACT.Exp, bias=st[:, 24 + c:25 + c], scale=SCALE,
                                   accum_out=st[:, 32 + c:33 + c]).then_inc(probs, 1)

            def stage_b(g):
                q, k, v, z = (slab("B", c, g) for c in "qkvz")
                act.wait_ge(y_lo_ready, 2 + g)
                his(q + 1, [0, 1])
                copy_bank(q, 0, W[:, 0, 0:512], q_rows)
                his(q + 1, [2, 3])
                copy_bank(q, 1, W[:, 0, 512:1024], q_rows)
                his(q + 2, [0, 1])
                copy_bank(k, 0, W[:, 1, 0:512], k_rows)
                his(q + 2, [2, 3])
                copy_bank(k, 1, W[:, 1, 512:1024], k_rows)
                his(q + 3, [0, 1, 2, 3])
                v_rows(v)
                his(q + 4, [0])
                softmax_exp(8 * 0 + 8 * g + 2, 0, True, g)
                softmax_exp(8 * g + 4, 1, True, g)
                his(q + 4, [1])
                silu_free(z, 0)
                softmax_exp(8 * g + 6, 2, True, g)
                softmax_exp(8 * g + 8, 3, True, g)
                his(q + 4, [2])
                for h in range(4):
                    act.wait_ge(probs_turned, 4 * g + h + 1)
                    act.activation(wview(4, 2)[:, 384 * h:384 * h + 384], head[h][:, 0:384], ACT.Copy
                                   ).then_inc(probsT_ready, 1)
                his(q + 4, [3])
                silu_free(z, 1)
                y_high(2 + g, 2 + g)

            def cross(layer):
                X = f"XA{layer}"
                nk, nq, nv, no = (slab(X, c) for c in "kqvo")
                base = 16 + 8 * layer
                if layer == 0:
                    his(nk + 1, [0, 1])
                    copy_bank(nk, 0, kx[:, 0:2, :].rearrange("p h t -> p (h t)"), k_rows)
                    his(nk + 1, [2, 3])
                    copy_bank(nk, 1, kx[:, 2:4, :].rearrange("p h t -> p (h t)"), k_rows)
                else:
                    his(nv + 1, [0, 1, 2, 3])
                    v_rows(nv)
                norm_high(1 + 2 * layer, "xa_norm", KC * layer)
                if nq + 1 < NSLAB:
                    his(nq + 1, [0, 1])
                copy_bank(nq, 0, W[:, 0, 0:512], q_rows)
                his(nq + 1, [2, 3])
                copy_bank(nq, 1, W[:, 0, 512:1024], q_rows)
                if layer == 0:
                    his(nv + 1, [0])
                for h in range(4):
                    softmax_exp(base + 2 * h + 2, h, False, 0)
                if layer == 0:
                    his(nv + 1, [1, 2, 3])
                    v_rows(nv)
                for h in range(4):
                    act.wait_ge(probs_turned, 8 + 4 * layer + h + 1)
                    act.activation(wview(4, 2)[:, 512 * h:512 * h + 512], head[h][:], ACT.Copy
                                   ).then_inc(probsT_ready, 1)
                for u in range(2):
                    act.wait_ge(o_psum, 8 + 2 * layer + (4 if layer else 0) + u + 1)
                    act.activation(y_hi[:, 2 * u:2 * u + 2, :], head[u][:].rearrange("p (h t) -> p h t", h=2), ACT.Copy
                                   ).then_inc(y_hi_ready, 1)

            def norm_high(i, gain, gk):
                act.wait_ge(x_added, 4 * i)
                square_sums(x_sb, wview(4))
                root(i + 1)
                xT_high(i, gain, gk)

            stage_a(0)
            stage_a(1)
            stage_b(0)
            stage_b(1)
            o0 = slab("OUT0", (0, 0))
            his(o0 + 1, range(4))
            his(o0 + 2, range(4))
            his(o0 + 3, range(4))
            act.wait_ge(quarter_used, 4 * (o0 + 3))
            mn_high(0, 0)
            his(o0 + 4, range(4))
            cross(0)
            act.wait_ge(quarter_used, 4 * (slab("XA0", "v") + 1))
            mn_high(1, 1)
            n = slab("XA1", "k")
            his(n, range(4))
            his(n + 1, [0])
            copy_bank(n, 0, kx[:, 0:2, :].rearrange("p h t -> p (h t)"), k_rows)
            his(n + 1, [1, 2])
            copy_bank(n, 1, kx[:, 2:4, :].rearrange("p h t -> p (h t)"), k_rows)
            his(n + 1, [3])
            norm_high(2, "od_norm", 0)

            def stage_c(g):
                cx, z = slab("C", "x", g), slab("C", "z", g)
                cxp = wview(0, 2)[:, 0:4 * (S + 3)].rearrange("p (h t) -> p h t", h=4)
                if g:
                    act.wait_ge(y_lo_ready, 6 + g)
                his(cx + 1, [0, 1])
                for u in range(2):
                    filled(act, cx, u)
                    act.activation(cxp[:, 2 * u:2 * u + 2, 3:S + 3], bank(cx, u)[:].rearrange("p (h t) -> p h t", h=2),
                                   ACT.Copy).then_inc(cx_ready, 1)
                    act.drain().then_inc(free_of(cx, u), 1)
                    if u == 0:
                        his(cx + 1, [2, 3])
                his(cx + 2, [0, 1])
                silu_free(z, 0)
                his(cx + 2, [2, 3])
                silu_free(z, 1)
                for m, (name, s) in enumerate((("od_rg_ba", rgate_ready), ("od_rg_bx", igate_ready))):
                    for h in range(4):
                        if h % 2 == 0:
                            act.wait_ge(gates_psum, 4 * g + 2 * m + h // 2 + 1)
                        last = act.activation(blocks(3 + m)[:, h, :], head[2 * m + h // 2][:, S * (h % 2):S * (h % 2) + S],
                                              ACT.Sigmoid, bias=param(name, 4 * g + h))
                    last.then_inc(s, 1)
                act.drain()
                act.wait_ge(soft_ready, 1)
                for h in range(4):
                    act.activation(blocks(5)[:, h, :], blocks(3)[:, h, :], ACT.Exp,
                                   scale=soft[:, 7, 4 * g + h:4 * g + h + 1])
                for h in range(4):
                    last = act.activation(blocks(0)[:, h, :], blocks(3)[:, h, :], ACT.Tanh,
                                          scale=soft[:, 6, 4 * g + h:4 * g + h + 1])
                last.then_inc(decay_ready, 1)
                act.wait_ge(one_minus, g + 1)
                act.activation(wview(0), wview(0), ACT.Sqrt).then_inc(root_ready, 1)
                y_high(4 + g, g)

            def stage_d(g):
                q, k, v, z = (slab("D", c, g) for c in "qkvz")
                his(q + 1, [0, 1, 2])
                his(q + 1, [3])
                his(q + 2, range(4))
                his(q + 3, [0])
                for h in range(2):
                    dm(g, h)
                his(q + 3, [1, 2, 3])
                v_rows(v)
                his(q + 4, [0])
                for h in range(2, 4):
                    dm(g, h)
                his(q + 4, [1])
                silu_free(z, 0)
                for u in range(2):
                    act.wait_ge(o_psum, 10 + 2 * g + u + 1)
                    act.activation(W[:, 4, 512 * u:512 * u + 512], head[u][:], ACT.Copy).then_inc(o_copied, 1)
                his(q + 4, [2])
                for u in range(2):
                    act.wait_ge(cen_psum, 2 * g + u + 1)
                    act.activation(W[:, 5, 512 * u:512 * u + 512], head[2 + u][:], ACT.Square).then_inc(o_square, 1)
                his(q + 4, [3])
                silu_free(z, 1)
                for u in range(2):
                    act.wait_ge(ms_psum, 4 + 2 * g + u + 1)
                    act.activation(W[:, 0, 512 * u:512 * u + 512], head[u][:], ACT.Ln, bias=st[:, 60:61])
                act.drain()
                act.activation(wview(0), wview(0), ACT.Exp, scale=-0.5).then_inc(o_rstd, 1)
                y_high(6 + g, 2 + g)

            def dm(g, h):
                i = 4 * g + h
                if i >= 2:
                    act.wait_ge(att_ready, 8 + i - 1)
                act.activation(dmask[:, h % 2, :], dist[:], ACT.Exp, scale=const[:, C_LOG_G + i:C_LOG_G + i + 1],
                               bias=st[:, 61:62]).then_inc(dmask_ready, 1)

            for g in range(2):
                stage_c(g)
            for g in range(2):
                stage_d(g)
            o1 = slab("OUT1", (0, 0))
            his(o1 + 1, range(4))
            his(o1 + 2, range(4))
            his(o1 + 3, range(4))
            act.wait_ge(quarter_used, 4 * (o1 + 3))
            mn_high(1, 2)
            his(o1 + 4, range(4))
            cross(1)
            act.wait_ge(x_added, 16)
            square_sums(x_sb, wview(4))
            root(5)

        @block.vector
        def _(dve):
            def lo(n, q):
                dve.wait_ge(hi_ready, 4 * n + q + 1)
                dve.tensor_tensor(ring_quarter(w_lo, n, q), raw_quarter(n, q),
                                  ring_quarter(w_hi, n, q).bitcast(F32), ALU.subtract).then_inc(lo_ready, 1)

            def los(n, qs):
                if n < NSLAB:
                    for q in qs:
                        lo(n, q)

            def norm_rows(i, src, dst):
                dve.wait_ge(sumsq, 2 * (i + 1))
                dve.tensor_scalar(st[:, 2:4], st[:, 0:2], 1.0 / D, EPS, ALU.mult, ALU.add)
                dve.drain()
                dve.reciprocal(st[:, 2:4], st[:, 2:4]).then_inc(inv_ready, 1)
                dve.wait_ge(rstd_ready, i + 1)
                for t in range(T):
                    last = dve.tensor_scalar(dst[:, t, :], src[:, t, :], st[:, 4 + t:5 + t], None, ALU.mult)
                last.then_inc(normed, 1)

            def xT_low(i, gain, gk):
                for k in range(KC):
                    dve.wait_ge(xT_hi_ready, KC * i + k - k % 2 + 2)
                    dve.scalar_tensor_tensor(out=xT_lo[:, k, :], in0=head[k // 2][:, S * (k % 2):S * (k % 2) + S],
                                             scalar=param(gain, gk + k), in1=xT_hi[:, k, :].bitcast(F32),
                                             op0=ALU.mult, op1=ALU.subtract).then_inc(xT_lo_ready, 1)

            def mn_low(layer, use):
                for k in range(KC):
                    dve.wait_ge(mn_hi_ready, KC * use + k + 1)
                    dve.scalar_tensor_tensor(out=y_lo[:, KC + k, :], in0=memT[:, k, :],
                                             scalar=param("xa_mem_norm", KC * layer + k),
                                             in1=y_hi[:, KC + k, :].bitcast(F32),
                                             op0=ALU.mult, op1=ALU.subtract).then_inc(mn_lo_ready, 1)

            def add_turn(n, c, half=0):
                for t in range(T):
                    filled(dve, n, t, half)
                    dve.tensor_tensor(x_sb[:, t, 512 * c:512 * c + 512], bank(n, t, half)[:],
                                      x_sb[:, t, 512 * c:512 * c + 512], ALU.add).then_inc(x_added, 1)
                    dve.drain().then_inc(free_of(n, t, half), 1)

            dve.memset(st[:, 60:61], EPS)
            dve.memset(st[:, 61:62], float(np.log(SCALE)))
            dve.wait_ge(mem_landed, 16)
            norm_rows(0, W[:, 2:4, :], W[:, 2:4, :])
            dve.wait_ge(x_landed, 16)
            norm_rows(1, x_sb, W[:, 0:2, :])
            dve.wait_ge(prm_ready, 1)
            los(0, [0, 1])
            xT_low(0, "ev_norm", 0)
            los(0, [2, 3])
            lg = prm[:, PARAM_AT["hgrn_lb_logits"]:PARAM_AT["hgrn_lb_logits"] + 3 * KC].rearrange(
                "p (j k) -> p j k", j=3)
            dve.tensor_tensor(lbp[:, 3, :], lg[:, 0, :], lg[:, 1, :], ALU.max)
            dve.drain()
            dve.tensor_tensor(lbp[:, 3, :], lbp[:, 3, :], lg[:, 2, :], ALU.max)
            dve.drain()
            for j in range(3):
                last = dve.tensor_tensor(lbp[:, j, :], lg[:, j, :], lbp[:, 3, :], ALU.subtract)
            last.then_inc(lb_max, 1)
            lam = prm[:, PARAM_AT["od_rg_lambda"]:PARAM_AT["od_rg_lambda"] + KC]
            dve.tensor_scalar(soft[:, 0, :], lam, -1.0, None, ALU.mult)
            dve.drain()
            dve.tensor_tensor(soft[:, 1, :], lam, soft[:, 0, :], ALU.max).then_inc(soft_abs, 1)
            dve.wait_ge(lb_exp, 1)
            dve.tensor_tensor(lbp[:, 3, :], lbp[:, 0, :], lbp[:, 1, :], ALU.add)
            dve.drain()
            dve.tensor_tensor(lbp[:, 3, :], lbp[:, 3, :], lbp[:, 2, :], ALU.add)
            dve.drain()
            dve.reciprocal(lbp[:, 3, :], lbp[:, 3, :])
            dve.drain()
            dve.tensor_tensor(lbp[:, 4, :], lbp[:, 0, :], lbp[:, 3, :], ALU.mult)
            dve.drain()
            dve.tensor_scalar(lbp[:, 5, :], lbp[:, 4, :], -1.0, 1.0, ALU.mult, ALU.add)

            def angles():
                pos = W[:, 5, S:2 * S]
                ang = trig
                k = wview(4).rearrange("p (a t) -> p a t", a=4)
                dve.wait_ge(pos_landed, 32)
                dve.tensor_copy(pos, W[:, 5, 0:S].bitcast(I32))
                dve.drain()
                for j, c in enumerate((C_INV_RET, C_INV_MOBA)):
                    dve.tensor_scalar(ang[:, 2 * j + 1, :], pos, const[:, c:c + 1], None, ALU.mult)
                dve.drain()
                sn = ang[:, 1:4:2, :]
                cs = ang[:, 0:3:2, :]
                kk = k[:, 0:2, :]
                dve.tensor_scalar(kk, sn, float(1 / (2 * np.pi)), ROUND, ALU.mult, ALU.add)
                dve.drain()
                dve.tensor_scalar(kk, kk, ROUND, None, ALU.subtract)
                dve.drain()
                for c in (TWO_PI_A, TWO_PI_B, TWO_PI_C):
                    dve.scalar_tensor_tensor(out=sn, in0=kk, scalar=-c, in1=sn, op0=ALU.mult, op1=ALU.add)
                    dve.drain()
                dve.tensor_scalar(cs, sn, float(np.pi / 2), None, ALU.add)
                dve.drain()
                dve.tensor_scalar(kk, cs, float(np.pi), -2 * float(np.pi), ALU.is_gt, ALU.mult)
                dve.drain()
                dve.tensor_tensor(cs, cs, kk, ALU.add)
                dve.drain()
                dve.tensor_scalar(trig[:], trig[:], PI_IN, -PI_IN, ALU.min, ALU.max).then_inc(angles_ready, 1)

            def softplus():
                dve.wait_ge(soft_exp, 1)
                e, s, s2, p = (soft[:, j, :] for j in (2, 3, 4, 5))
                dve.tensor_scalar(s, e, 2.0, None, ALU.add)
                dve.drain()
                dve.reciprocal(s, s)
                dve.drain()
                dve.tensor_tensor(s, s, e, ALU.mult)
                dve.drain()
                dve.tensor_tensor(s2, s, s, ALU.mult)
                dve.drain()
                dve.tensor_scalar(p, s2, 1.0 / 15, None, ALU.mult)
                dve.drain()
                for c in (13, 11, 9, 7, 5, 3):
                    dve.scalar_tensor_tensor(out=p, in0=p, scalar=1.0 / c, in1=s2, op0=ALU.add, op1=ALU.mult)
                    dve.drain()
                dve.scalar_tensor_tensor(out=p, in0=p, scalar=1.0, in1=s, op0=ALU.add, op1=ALU.mult)
                dve.tensor_scalar(soft[:, 0, :], soft[:, 0, :], 0.0, None, ALU.max)
                dve.drain()
                dve.scalar_tensor_tensor(out=p, in0=p, scalar=2.0, in1=soft[:, 0, :], op0=ALU.mult, op1=ALU.add)
                dve.drain()
                dve.tensor_scalar(soft[:, 6, :], p, RG_C, None, ALU.mult)
                dve.tensor_scalar(soft[:, 7, :], p, -RG_C, None, ALU.mult).then_inc(soft_ready, 1)

            def sign_trig():
                dve.wait_ge(trig_ready, 1)
                dve.tensor_scalar(trig[:, 1, :], trig[:, 1, :], const[:, C_SIGN_RET:C_SIGN_RET + 1], None, ALU.mult)
                dve.tensor_scalar(trig[:, 3, :], trig[:, 3, :], const[:, C_SIGN_MOBA:C_SIGN_MOBA + 1], None, ALU.mult)

            def stage_a(g):
                f, q, i, z = (slab("A", c, g) for c in "fqiz")
                los(f + 1, [0])

                def forget(u):
                    dve.wait_ge(f_sig, 2 * g + u + 1)
                    for h in (2 * u, 2 * u + 1):
                        dve.tensor_scalar(blocks(0)[:, h, :], blocks(0)[:, h, :], lbp[:, 5, 4 * g + h:4 * g + h + 1],
                                          lbp[:, 4, 4 * g + h:4 * g + h + 1], ALU.mult, ALU.add)

                forget(0)
                los(f + 1, [1, 2])
                forget(1)
                dve.drain()
                dve.tensor_scalar(wview(1), wview(0), -1.0, 1.0, ALU.mult, ALU.add).then_inc(f_ready, 1)
                los(f + 1, [3])
                dve.wait_ge(lnf_ready, g + 1)
                if g == 0:
                    dve.wait_ge(masks_ready, 2)
                dve.tensor_tensor_scan(wview(2), scan_mask[:], wview(0), 0.0, ALU.mult, ALU.add).then_inc(b_ready, 1)
                dve.drain()
                los(f + 2, [0])
                bc = wview(2).rearrange("p (c s) -> p c s", s=HGRN_CHUNK)
                dve.tensor_tensor(wview(5).rearrange("p (c s) -> p c s", s=HGRN_CHUNK),
                                  bc[:, :, HGRN_CHUNK - 1:HGRN_CHUNK].broadcast_to([P, 4 * NCH, HGRN_CHUNK]), bc, ALU.subtract
                                  ).then_inc(bend_ready, 1)
                los(f + 2, [1])
                dve.wait_ge(exps_ready, 2 * g + 2)
                dve.tensor_tensor(wview(0), wview(1), wview(0), ALU.mult).then_inc(kinv_ready, 1)
                los(f + 2, [2])
                dve.wait_ge(eend_ready, g + 1)
                dve.tensor_tensor(wview(1), wview(1), wview(5), ALU.mult).then_inc(kend_ready, 1)
                for u in range(2):
                    filled(dve, q, u)
                    dve.tensor_tensor(W[:, 4, 512 * u:512 * u + 512], bank(q, u)[:], W[:, 3, 512 * u:512 * u + 512],
                                      ALU.mult).then_inc(qdec_ready, 1)
                    dve.drain().then_inc(free_of(q, u), 1)
                los(f + 2, [3])
                los(f + 3, [0, 1])
                for h in range(4):
                    dve.wait_ge(att_psum, 2 * g + h // 2 + 1)
                    for t in range(T):
                        c = S * (h % 2) + P * t
                        last = dve.copy_predicated(att[:, h, P * t:P * t + P], chunk_mask[:],
                                                   head[h // 2][:, c:c + P])
                    last.then_inc(att_ready, 1)
                los(f + 3, [2, 3])

                def chain(h):
                    for c in range(NCH - 1):
                        u = head[c % 4][:, P * (2 * (h % 2) + c // 4):P * (2 * (h % 2) + c // 4) + P]
                        if c == 0:
                            last = dve.tensor_copy(states[:, h, 0, :], u)
                        else:
                            col = S * h + HGRN_CHUNK * c + HGRN_CHUNK - 1
                            dve.drain()
                            last = dve.scalar_tensor_tensor(out=states[:, h, c, :], in0=states[:, h, c - 1, :],
                                                            scalar=W[:, 3, col:col + 1], in1=u, op0=ALU.mult,
                                                            op1=ALU.add)
                    last.then_inc(state_ready, 1)

                los(f + 4, [0])
                dve.wait_ge(u_psum, 2 * g + 1)
                chain(0)
                los(f + 4, [1])
                chain(1)
                los(f + 4, [2])
                dve.wait_ge(u_psum, 2 * g + 2)
                chain(2)
                los(f + 4, [3])
                chain(3)
                gated(g, g, 0, 2 * g, None)

            def gated(i, G, dst, zi, bias):
                dve.wait_ge(o_rstd, i + 1)
                dve.wait_ge(z_ready, 2 * (i + 1))
                for h in range(4):
                    dve.scalar_tensor_tensor(out=blocks(dst)[:, h, :], in0=head[h // 2][:, S * (h % 2):S * (h % 2) + S],
                                             scalar=param("ev_hgrn_gain", 4 * G + h), in1=blocks(5)[:, h, :],
                                             op0=ALU.mult, op1=ALU.mult)
                dve.drain()
                dve.tensor_tensor(wview(dst), wview(dst), zs[:].rearrange("p h t -> p (h t)"), ALU.mult
                                  ).then_inc(y_ready, 1)

            def rope_moba(w, ready, done, cnt):
                dve.wait_ge(ready, cnt)
                mask = [(j + 16) % 32 for j in range(32)]
                x32 = blocks(w)[0:32, :, :]
                t32 = blocks(2)[0:32, :, :]
                cos = trig[0:32, 2:3, :].broadcast_to([32, 4, S])
                sin = trig[0:32, 3:4, :].broadcast_to([32, 4, S])
                dve.drain()
                dve.stream_shuffle(W[0:32, 2, :], W[0:32, w, :], mask)
                dve.drain()
                dve.tensor_tensor(t32, t32, sin, ALU.mult)
                dve.tensor_tensor(x32, x32, cos, ALU.mult)
                dve.drain()
                dve.tensor_tensor(x32, x32, t32, ALU.add).then_inc(done, 1)

            def softmax_max(i, h, moba):
                dve.wait_ge(scores, i)
                for t in range(T):
                    c = 2 * h + t
                    if moba:
                        a, b = 128 * t, 128 + 256 * t
                        sc = wview(2, 2)[:, 384 * h + a:384 * h + b]
                        last = dve.tensor_tensor_reduce(out=sc, in0=head[h][:, a:b], in1=causal[:, a:b], scale=1.0,
                                                        scalar=3 * NEG, op0=ALU.add, op1=ALU.max,
                                                        accum_out=st[:, 16 + c:17 + c])
                if not moba:
                    dve.tensor_reduce(st[:, 16 + 2 * h:18 + 2 * h], head[h][:].rearrange("p (t k) -> p t k", t=2),
                                      AX_X, ALU.max)
                dve.drain()
                dve.tensor_scalar(st[:, 24 + 2 * h:26 + 2 * h], st[:, 16 + 2 * h:18 + 2 * h], -SCALE, None, ALU.mult
                                  ).then_inc(row_max, 2)

            def softmax_norm(i, h, moba):
                dve.wait_ge(probs, i)
                dve.reciprocal(st[:, 40 + 2 * h:42 + 2 * h], st[:, 32 + 2 * h:34 + 2 * h])
                dve.drain()
                for t in range(T):
                    c = 40 + 2 * h + t
                    pr = (wview(2, 2)[:, 384 * h + 128 * t:384 * h + 128 + 256 * t] if moba else
                          wview(2, 2)[:, 512 * h + 256 * t:512 * h + 256 * t + 256])
                    last = dve.tensor_scalar(pr, pr, st[:, c:c + 1], None, ALU.mult)
                last.then_inc(probs_norm, 1)

            def stage_b(g):
                q, k, v, z = (slab("B", c, g) for c in "qkvz")
                los(q + 1, [0, 1, 2, 3])
                rope_moba(0, q_rows, q_ready, 2 * g + 2)
                los(q + 2, [0, 1, 2, 3])
                rope_moba(1, k_rows, k_ready, 2 * g + 2)
                los(q + 3, [0, 1])
                for h in range(4):
                    softmax_max(4 * g + h + 1, h, True)
                los(q + 3, [2, 3])
                los(q + 4, [0])
                softmax_norm(8 * g + 2, 0, True)
                softmax_norm(8 * g + 4, 1, True)
                los(q + 4, [1])
                softmax_norm(8 * g + 6, 2, True)
                softmax_norm(8 * g + 8, 3, True)
                los(q + 4, [2, 3])
                dve.wait_ge(z_ready, 2 * (3 + g))
                for u in range(2):
                    dve.wait_ge(o_psum, 4 + 2 * g + u + 1)
                    last = dve.tensor_tensor(W[:, 0, 512 * u:512 * u + 512], head[u][:],
                                             zs[:, 2 * u:2 * u + 2, :].rearrange("p h t -> p (h t)"), ALU.mult)
                last.then_inc(y_ready, 1)

            def norm_low(i, gain, gk):
                dve.wait_ge(x_added, 4 * i)
                norm_rows(i + 1, x_sb, W[:, 0:2, :])
                xT_low(i, gain, gk)

            def cross(layer):
                X = f"XA{layer}"
                nk, nq, nv, no = (slab(X, c) for c in "kqvo")
                base = 16 + 8 * layer
                if layer == 0:
                    los(nk + 1, range(4))
                else:
                    los(nv + 1, range(4))
                norm_low(1 + 2 * layer, "xa_norm", KC * layer)
                if nq + 1 < NSLAB:
                    los(nq + 1, range(4))
                for h in range(4):
                    softmax_max(8 + 4 * layer + h + 1, h, False)
                if layer == 0:
                    los(nv + 1, [0])
                for h in range(4):
                    softmax_norm(base + 2 * h + 2, h, False)
                if layer == 0:
                    los(nv + 1, [1, 2, 3])
                for u in range(2):
                    i = (4 if layer == 0 else 10) + u + 1
                    dve.wait_ge(y_hi_ready, i)
                    dve.tensor_tensor(y_lo[:, 2 * u:2 * u + 2, :], head[u][:].rearrange("p (h t) -> p h t", h=2),
                                      y_hi[:, 2 * u:2 * u + 2, :].bitcast(F32), ALU.subtract).then_inc(y_lo_ready, 1)

            angles()
            softplus()
            stage_a(0)
            sign_trig()
            stage_a(1)
            stage_b(0)
            stage_b(1)
            o0 = slab("OUT0", (0, 0))
            los(o0 + 1, range(4))
            los(o0 + 2, range(4))
            add_turn(o0 + 1, 0)
            los(o0 + 3, range(4))
            mn_low(0, 0)
            los(o0 + 4, range(4))
            add_turn(o0 + 3, 1)
            cross(0)
            mn_low(1, 1)
            n = slab("XA1", "k")
            los(n, [0, 1])
            add_turn(slab("XA0", "o"), 0, 0)
            los(n, [2, 3])
            add_turn(slab("XA0", "o"), 1, 1)
            los(n + 1, range(4))
            norm_low(2, "od_norm", 0)

            def stage_c(g):
                cx, z = slab("C", "x", g), slab("C", "z", g)
                cxp = wview(0, 2)[:, 0:4 * (S + 3)].rearrange("p (h t) -> p h t", h=4)
                if g:
                    dve.wait_ge(y_lo_ready, 4 + 2 + g)
                dve.memset(cxp[:, :, 0:3], 0.0)
                los(cx + 1, range(4))
                for u in range(2):
                    dve.wait_ge(cx_ready, 2 * g + u + 1)
                    dve.drain()
                    for h in (2 * u, 2 * u + 1):
                        dve.tensor_scalar(blocks(2)[:, h, :], cxp[:, h, 0:S], param("od_conv_w", 4 * g + h),
                                          param("od_conv_b", 4 * g + h), ALU.mult, ALU.add)
                    for j in range(1, 4):
                        dve.drain()
                        for h in (2 * u, 2 * u + 1):
                            last = dve.scalar_tensor_tensor(out=blocks(2)[:, h, :], in0=cxp[:, h, j:j + S],
                                                            scalar=param("od_conv_w", KC * j + 4 * g + h),
                                                            in1=blocks(2)[:, h, :], op0=ALU.mult, op1=ALU.add)
                    last.then_inc(xf_ready, 1)
                    if u == 0:
                        los(cx + 2, [0, 1])
                los(cx + 2, [2, 3])
                dve.drain()
                dve.wait_ge(igate_ready, g + 1)
                dve.tensor_tensor(wview(4), wview(4), wview(2), ALU.mult)
                dve.wait_ge(decay_ready, g + 1)
                dve.tensor_tensor(wview(1), wview(5), wview(5), ALU.mult)
                dve.drain()
                dve.scalar_tensor_tensor(out=wview(0), in0=wview(1), scalar=1.0, in1=wview(0), op0=ALU.add,
                                         op1=ALU.mult).then_inc(one_minus, 1)
                dve.memset(blocks(5)[:, :, 0:1], 0.0)
                dve.wait_ge(root_ready, g + 1)
                dve.tensor_tensor(wview(4), wview(4), wview(0), ALU.mult)
                dve.drain()
                dve.tensor_tensor_scan(wview(1), wview(5), wview(4), 0.0, ALU.mult, ALU.add)
                dve.drain()
                dve.wait_ge(z_ready, 8 + 2 * (g + 1))
                dve.tensor_tensor(wview(1), wview(1), zs[:].rearrange("p h t -> p (h t)"), ALU.mult
                                  ).then_inc(y_ready, 1)

            def rope_full(n, w, done):
                for u in range(2):
                    filled(dve, n, u)
                    src = bank(n, u)[:].rearrange("p (h t) -> p h t", h=2)
                    cos = trig[:, 0:1, :].broadcast_to([P, 2, S])
                    dst = blocks(w)[:, 2 * u:2 * u + 2, :]
                    tmp = blocks(5)[:, 2 * u:2 * u + 2, :]
                    for a, b in ((0, 64), (64, 0)):
                        dve.tensor_tensor(tmp[a:a + 64], src[b:b + 64], trig[b:b + 64, 1:2, :].broadcast_to([64, 2, S]), ALU.mult)
                    dve.tensor_tensor(dst, src, cos, ALU.mult)
                    dve.drain().then_inc(free_of(n, u), 1)
                    dve.tensor_tensor(dst, dst, tmp, ALU.add).then_inc(done, 1)

            def stage_d(g):
                q, k, v, z = (slab("D", c, g) for c in "qkvz")
                los(q + 1, [0, 1, 2, 3])
                dve.wait_ge(y_lo_ready, 6 + 2 + g)
                rope_full(q, 0, q_ready)
                los(q + 2, [0, 1, 2, 3])
                rope_full(k, 1, k_ready)
                los(q + 3, [0, 1])
                los(q + 3, [2, 3])
                for h in range(4):
                    if h == 2:
                        los(q + 4, [0])
                    i = 4 * g + h
                    dve.wait_ge(dmask_ready, i + 1)
                    dve.wait_ge(att_psum, 4 + i + 1)
                    dve.tensor_tensor(wview(2, 2)[:, 384 * h:384 * h + 384], head[h][:, 0:384], dmask[:, h % 2, :],
                                      ALU.mult).then_inc(att_ready, 1)
                los(q + 4, [1, 2, 3])
                dve.wait_ge(o_rstd, 3 + g)
                for h in range(4):
                    dve.scalar_tensor_tensor(out=blocks(1)[:, h, :], in0=head[2 + h // 2][:, S * (h % 2):S * (h % 2) + S],
                                             scalar=param("od_ret_gain", 4 * g + h), in1=blocks(0)[:, h, :],
                                             op0=ALU.mult, op1=ALU.mult)
                dve.drain()
                dve.wait_ge(z_ready, 12 + 2 * (g + 1))
                for h in range(4):
                    last = dve.scalar_tensor_tensor(out=blocks(1)[:, h, :], in0=blocks(1)[:, h, :],
                                                    scalar=param("od_ret_bias", 4 * g + h), in1=zs[:, h, :],
                                                    op0=ALU.add, op1=ALU.mult)
                last.then_inc(y_ready, 1)

            for g in range(2):
                stage_c(g)
            for g in range(2):
                stage_d(g)
            o1 = slab("OUT1", (0, 0))
            los(o1 + 1, range(4))
            los(o1 + 2, range(4))
            add_turn(o1 + 1, 0)
            los(o1 + 3, range(4))
            mn_low(1, 2)
            los(o1 + 4, range(4))
            add_turn(o1 + 3, 1)
            cross(1)
            add_turn(slab("XA1", "o"), 0, 0)
            add_turn(slab("XA1", "o"), 1, 1)
            dve.wait_ge(sumsq, 12)
            dve.tensor_scalar(st[:, 2:4], st[:, 0:2], 1.0 / D, EPS, ALU.mult, ALU.add)
            dve.drain()
            dve.reciprocal(st[:, 2:4], st[:, 2:4]).then_inc(inv_ready, 1)
            dve.wait_ge(rstd_ready, 6)
            dve.wait_ge(fgain_landed, 16)
            for t in range(T):
                dve.scalar_tensor_tensor(out=x_sb[:, t, :], in0=x_sb[:, t, :], scalar=st[:, 4 + t:5 + t], in1=fgain,
                                         op0=ALU.mult, op1=ALU.mult).then_inc(fin_ready, 1)

        @block.tensor
        def _(pe):
            def split_ready(n, q):
                pe.wait_ge(hi_ready, 4 * n + q + 1)
                pe.wait_ge(lo_ready, 4 * n + q + 1)

            def take_bank(n, u, half=0):
                before = (TURN[n] + half) // 2
                if before >= 1:
                    pe.wait_ge(free_of(n, u, half), before)

            def quarter_f(n, q, x_hi, x_lo, k0=0):
                if q % 2 == 0:
                    take_bank(n, q // 2)
                split_ready(n, q)
                dst = bank(n, q // 2)[:, S * (q % 2):S * (q % 2) + S]
                wh, wl = ring_quarter(w_hi, n, q), ring_quarter(w_lo, n, q)
                for k in range(KC):
                    pe.matmul(dst, wh[:, k, :], x_hi[:, k0 + k, :], start=(k == 0), stop=False)
                    pe.matmul(dst, wh[:, k, :], x_lo[:, k0 + k, :], start=False, stop=False)
                    last = pe.matmul(dst, wl[:, k, :], x_hi[:, k0 + k, :], start=False, stop=(k == KC - 1))
                last.then_inc(quarter_used, 1)

            def quarter_t(n, q, x_hi, x_lo, k0, half=0, start=True, stop=True):
                first = start and (q % 2 == 0 if SLABS[n][2] == "W" else q == 0)
                final = stop and (q % 2 == 1 if SLABS[n][2] == "W" else q == 3)
                if first:
                    for t in range(T):
                        take_bank(n, t, half)
                split_ready(n, q)
                wh, wl = ring_quarter(w_hi, n, q), ring_quarter(w_lo, n, q)
                for t in range(T):
                    dst = bank(n, t, half)[:]
                    tok = slice(P * t, P * t + P)
                    for k in range(2):
                        pe.matmul(dst, x_hi[:, k0 + k, tok], wh[:, k, :], start=first and k == 0, stop=False)
                        pe.matmul(dst, x_lo[:, k0 + k, tok], wh[:, k, :], start=False, stop=False)
                        last = pe.matmul(dst, x_hi[:, k0 + k, tok], wl[:, k, :], start=False, stop=final and k == 1)
                last.then_inc(quarter_used, 1)

            def slab_f(n, qs=range(4), x=(xT_hi, xT_lo), k0=0):
                for q in qs:
                    quarter_f(n, q, x[0], x[1], k0)

            def slab_t(n, qs=range(4), x=(xT_hi, xT_lo), k0=0, start=True, stop=True):
                for q in qs:
                    quarter_t(n, q, x[0], x[1], k0 + 2 * q, start=start, stop=stop)

            def turn_rows(src):
                for k in range(KC):
                    for t in range(T):
                        last = pe.transpose(head[k // 2][:, S * (k % 2) + P * t:S * (k % 2) + P * t + P],
                                            src[:, t, P * k:P * k + P], ident[:])
                    if k % 2:
                        last.then_inc(turned, 1)

            pe.wait_ge(masks_ready, 1)
            pe.wait_ge(prm_landed, 16 * len(PARAM_ROWS))
            pe.transpose(proj[0][:, 0:P], prm_rows[:, 0, :], ident[:])
            pe.transpose(proj[0][:, P:N_ROWS], prm_rows[0:N_ROWS - P, 1, :], ident[0:N_ROWS - P, 0:N_ROWS - P]
                         ).then_inc(prm_turned, 1)
            pe.wait_ge(normed, 1)
            turn_rows(W[:, 2:4, :])
            pe.wait_ge(normed, 2)
            pe.wait_ge(memT_ready, 4)
            turn_rows(W[:, 0:2, :])
            pe.wait_ge(prm_ready, 1)
            pe.wait_ge(xT_hi_ready, KC)
            pe.wait_ge(xT_lo_ready, KC)

            def stage_a(g):
                f, q, i, z = (slab("A", c, g) for c in "fqiz")
                slab_f(f)
                slab_f(q)
                slab_t(i, [0, 1])
                pe.wait_ge(kinv_ready, g + 1)
                pe.wait_ge(qdec_ready, 2 * g + 2)
                if g:
                    pe.wait_ge(y_ready, g)
                for h in range(4):
                    for t in range(T):
                        c = S * h + P * t
                        last = pe.matmul(head[h // 2][:, S * (h % 2) + P * t:S * (h % 2) + P * t + P],
                                         W[:, 0, c:c + P], W[:, 4, c:c + P], start=True, stop=True)
                    if h % 2:
                        last.then_inc(att_psum, 1)
                pe.wait_ge(kend_ready, g + 1)
                for t in range(T):
                    for h in range(4):
                        last = pe.transpose(head[2 + t][:, P * h:P * h + P], W[:, 1, S * h + P * t:S * h + P * t + P],
                                            ident[:])
                    last.then_inc(kend_turned, 1)
                slab_t(i, [2, 3])
                slab_f(z, [0])

                def own_states(h0):
                    for h in (h0, h0 + 1):
                        for c in range(NCH - 1):
                            t, j = divmod(c, 4)
                            r = slice(HGRN_CHUNK * j, HGRN_CHUNK * j + HGRN_CHUNK)
                            last = pe.matmul(head[j][:, P * (2 * (h % 2) + t):P * (2 * (h % 2) + t) + P],
                                             kend_rows[r, t, h, :], v_sb[r, t, P * h:P * h + P], start=True, stop=True)
                    last.then_inc(u_psum, 1)

                pe.wait_ge(att_ready, 4 * g + 4)
                pe.wait_ge(kend_rows_ready, 2 * g + 2)
                pe.wait_ge(v_ready, 2 * g + 2)
                own_states(0)
                slab_f(z, [1, 2])
                pe.wait_ge(state_ready, 4 * g + 2)
                own_states(2)
                slab_f(z, [3])
                pe.wait_ge(state_ready, 4 * g + 4)
                for h in range(4):
                    dst = head[h // 2][:, S * (h % 2):S * (h % 2) + S]
                    for t in range(T):
                        pe.matmul(dst[:, P * t:P * t + P], v_sb[:, t, P * h:P * h + P], att[:, h, P * t:P * t + P],
                                  start=(t == 0), stop=False, skip_group_check=True)
                    for c in range(1, NCH):
                        last = pe.matmul(dst[:, HGRN_CHUNK * c:HGRN_CHUNK * c + HGRN_CHUNK], states[:, h, c - 1, :],
                                         W[:, 4, S * h + HGRN_CHUNK * c:S * h + HGRN_CHUNK * c + HGRN_CHUNK],
                                         start=False, stop=(c == NCH - 1), skip_group_check=True)
                    if h % 2:
                        last.then_inc(o_psum, 1)
                for u in range(2):
                    pe.wait_ge(o_square, 2 * g + u + 1)
                    pe.matmul(head[2 + u][:], avg[:], W[:, 1, 512 * u:512 * u + 512], start=True, stop=True
                              ).then_inc(ms_psum, 1)

            def values_out(h, spans):
                dst = head[h // 2][:, S * (h % 2):S * (h % 2) + S]
                for j, (t, a, w, src) in enumerate(spans):
                    last = pe.matmul(dst[:, a:a + w], v_sb[:, t, P * h:P * h + P], src, start=(j == 0),
                                     stop=(j == len(spans) - 1), skip_group_check=True)
                return last

            def stage_b(g):
                q, k, v, z = (slab("B", c, g) for c in "qkvz")
                slab_f(q)
                slab_f(k)
                slab_t(v, [0, 1])
                pe.wait_ge(q_ready, g + 1)
                pe.wait_ge(k_ready, g + 1)
                pe.wait_ge(y_ready, 2 + g)
                for h in range(4):
                    pe.matmul(head[h][:, 0:P], W[:, 0, S * h:S * h + P], W[:, 1, S * h:S * h + P],
                              start=True, stop=True)
                    pe.matmul(head[h][:, P:3 * P], W[:, 0, S * h + P:S * h + S], W[:, 1, S * h:S * h + S],
                              start=True, stop=True).then_inc(scores, 1)
                slab_t(v, [2, 3])
                slab_f(z, [0, 1])
                for h in range(4):
                    pe.wait_ge(probs_norm, 4 * g + h + 1)
                    for c in range(3):
                        last = pe.transpose(head[h][:, P * c:P * c + P], wview(2, 2)[:, 384 * h + P * c:384 * h + P * c + P],
                                            ident[:])
                    last.then_inc(probs_turned, 1)
                slab_f(z, [2, 3])
                pe.wait_ge(v_ready, 4 + 2 * g + 2)
                pe.wait_ge(probsT_ready, 4 * g + 4)
                for h in range(4):
                    pt = wview(4, 2)[:, 384 * h:384 * h + 384]
                    last = values_out(h, [(0, 0, S, pt[:, 0:S]), (1, P, P, pt[:, S:3 * P])])
                    if h % 2:
                        last.then_inc(o_psum, 1)

            def out_proj(stage, y_done):
                n = slab(stage, (0, 0))
                pe.wait_ge(y_hi_ready, y_done[0])
                pe.wait_ge(y_lo_ready, y_done[1])
                slab_t(n, x=(y_hi, y_lo), k0=0, stop=False)
                pe.wait_ge(y_hi_ready, y_done[0] + 2)
                pe.wait_ge(y_lo_ready, y_done[1] + 2)
                slab_t(n + 1, x=(y_hi, y_lo), k0=KC, start=False)
                slab_t(n + 2, x=(y_hi, y_lo), k0=KC, stop=False)
                slab_t(n + 3, x=(y_hi, y_lo), k0=0, start=False)

            def cross(layer):
                X = f"XA{layer}"
                nk, nq, nv, no = (slab(X, c) for c in "kqvo")
                use = 2 * layer
                pe.wait_ge(mn_hi_ready, KC * (use + 1))
                pe.wait_ge(mn_lo_ready, KC * (use + 1))
                if layer == 0:
                    slab_f(nk, x=(y_hi, y_lo), k0=KC)
                else:
                    slab_t(nv, x=(y_hi, y_lo), k0=KC)
                i = 1 + 2 * layer
                pe.wait_ge(normed, i + 2)
                turn_rows(W[:, 0:2, :])
                pe.wait_ge(xT_hi_ready, KC * (i + 1))
                pe.wait_ge(xT_lo_ready, KC * (i + 1))
                slab_f(nq)
                pe.wait_ge(k_rows, 6 + 2 * layer)
                for h in range(4):
                    pe.wait_ge(q_rows, 4 + 2 * layer + h // 2 + 1)
                    for t in range(T):
                        last = pe.matmul(head[h][:, S * t:S * t + S], W[:, 0, S * h + P * t:S * h + P * t + P],
                                         kx[:, h, :], start=True, stop=True)
                    last.then_inc(scores, 1)
                if layer == 0:
                    slab_t(nv, x=(y_hi, y_lo), k0=KC)
                for h in range(4):
                    pe.wait_ge(probs_norm, 8 + 4 * layer + h + 1)
                    for t in range(T):
                        for kt in range(T):
                            last = pe.transpose(head[h][:, S * kt + P * t:S * kt + P * t + P],
                                                wview(2, 2)[:, 512 * h + S * t + P * kt:512 * h + S * t + P * kt + P],
                                                ident[:])
                    last.then_inc(probs_turned, 1)
                pe.wait_ge(v_ready, (10 if layer == 0 else 16))
                for h in range(4):
                    if h == 0:
                        pe.wait_ge(probsT_ready, 8 + 4 * layer + 2)
                    pe.wait_ge(probsT_ready, 8 + 4 * layer + max(h + 1, 1))
                    pt = wview(4, 2)[:, 512 * h:512 * h + 512]
                    last = values_out(h, [(0, 0, S, pt[:, 0:S]), (1, 0, S, pt[:, S:2 * S])])
                    if h % 2:
                        last.then_inc(o_psum, 1)
                pe.wait_ge(y_lo_ready, 6 if layer == 0 else 12)
                for q in range(4):
                    quarter_t(no, q, y_hi, y_lo, 2 * (q % 2), half=q // 2)

            stage_a(0)
            stage_a(1)
            stage_b(0)
            stage_b(1)
            out_proj("OUT0", (2, 2))
            cross(0)
            pe.wait_ge(mn_hi_ready, 2 * KC)
            pe.wait_ge(mn_lo_ready, 2 * KC)
            slab_f(slab("XA1", "k"), x=(y_hi, y_lo), k0=KC)
            pe.wait_ge(normed, 4)
            turn_rows(W[:, 0:2, :])
            pe.wait_ge(xT_hi_ready, 3 * KC)
            pe.wait_ge(xT_lo_ready, 3 * KC)

            def stage_c(g):
                cx, z = slab("C", "x", g), slab("C", "z", g)
                slab_f(cx)
                slab_f(z, [0, 1, 2])
                pe.wait_ge(rg_landed[g], 32)
                for m in range(2):
                    for h in range(4):
                        if m == 0 and h % 2 == 0:
                            pe.wait_ge(xf_ready, 2 * g + h // 2 + 1)
                        if g and m == 0 and h == 0:
                            pe.wait_ge(igate_ready, g)
                        last = pe.matmul(head[2 * m + h // 2][:, S * (h % 2):S * (h % 2) + S], rg_w[:, 2 * g + m, h, :],
                                         blocks(2)[:, h, :], start=True, stop=True)
                        if h % 2:
                            last.then_inc(gates_psum, 1)
                slab_f(z, [3])

            def stage_d(g):
                q, k, v, z = (slab("D", c, g) for c in "qkvz")
                slab_f(q)
                slab_f(k)
                slab_t(v, [0, 1, 2])
                pe.wait_ge(q_ready, 2 + 2 * g + 2)
                pe.wait_ge(k_ready, 2 + 2 * g + 2)
                pe.wait_ge(y_ready, 6 + g)
                for h in range(4):
                    pe.matmul(head[h][:, 0:S], W[:, 1, S * h:S * h + P], W[:, 0, S * h:S * h + S],
                              start=True, stop=True)
                    pe.matmul(head[h][:, S:3 * P], W[:, 1, S * h + P:S * h + S], W[:, 0, S * h + P:S * h + S],
                              start=True, stop=True).then_inc(att_psum, 1)
                slab_t(v, [3])
                slab_f(z, [0, 1])
                pe.wait_ge(v_ready, 10 + 2 * g + 2)
                pe.wait_ge(att_ready, 8 + 4 * g + 4)
                for h in range(4):
                    am = wview(2, 2)[:, 384 * h:384 * h + 384]
                    last = values_out(h, [(0, 0, S, am[:, 0:S]), (1, P, P, am[:, S:3 * P])])
                    if h % 2:
                        last.then_inc(o_psum, 1)
                slab_f(z, [2])
                for u in range(2):
                    pe.wait_ge(o_copied, 2 * g + u + 1)
                    pe.matmul(head[2 + u][:], center[:], W[:, 4, 512 * u:512 * u + 512], start=True, stop=True
                              ).then_inc(cen_psum, 1)
                slab_f(z, [3])
                for u in range(2):
                    pe.wait_ge(o_square, 4 + 2 * g + u + 1)
                    pe.matmul(head[u][:], avg[:], W[:, 5, 512 * u:512 * u + 512], start=True, stop=True
                              ).then_inc(ms_psum, 1)

            for g in range(2):
                stage_c(g)
            for g in range(2):
                stage_d(g)
            out_proj("OUT1", (8, 8))
            cross(1)


def shape_constants():
    c = np.zeros((P, N_CONST), np.float32)
    p = np.arange(P)
    ret = np.float32(10000.0) ** (-(np.arange(64, dtype=np.float32)) / np.float32(64))
    moba = np.float32(500000.0) ** (-(np.arange(16, dtype=np.float32)) / np.float32(16))
    c[:, C_INV_RET] = ret[p % 64]
    c[:32, C_INV_MOBA] = moba[p[:32] % 16]
    c[:, C_SIGN_RET] = np.where(p < 64, 1.0, -1.0)
    c[:, C_SIGN_MOBA] = np.where(p < 16, -1.0, 1.0)
    c[:, C_LOG_G:C_LOG_G + 8] = np.log1p(-2.0 ** (-5.0 - np.arange(8.0)))[None, :]
    return c


_INS = ['x', 'mem', 'positions', 'hgrn_lb_logits', 'ev_norm', 'ev_w_in', 'ev_hgrn_gain', 'ev_w_out', 'od_norm',
        'od_w_in', 'od_conv_w', 'od_conv_b', 'od_rg_wa', 'od_rg_ba', 'od_rg_wx', 'od_rg_bx', 'od_rg_lambda',
        'od_ret_gain', 'od_ret_bias', 'od_w_out', 'xa_norm', 'xa_mem_norm', 'xa_wq', 'xa_wkv', 'xa_wo', 'final_norm']


def kernel(**inputs):
    import numpy as _np
    import concourse.bacc as _bacc
    from concourse import mybir as _mybir
    from concourse.bass_utils import run_bass_kernel_spmd as _run

    nc = _bacc.Bacc("TRN2", target_bir_lowering=False, num_devices=1)
    arrays, aps = {}, {}
    given = {name: _np.ascontiguousarray(inputs[name]) for name in _INS}
    given["shape_constants"] = shape_constants()
    for name, a in given.items():
        arrays[f"in_{name}_dram"] = a
        aps[name] = nc.dram_tensor(f"in_{name}_dram", a.shape, _mybir.dt.from_np(a.dtype), kind="ExternalInput").ap()
    out = nc.dram_tensor("out_0_dram", (1, S, D), F32, kind="ExternalOutput").ap()
    hybrid_trunk(nc, aps, out)
    r = _run(nc, [arrays], core_ids=[0])
    return r.results[0]["out_0_dram"]
```

```python
from contextlib import ExitStack

import numpy as np

import concourse.bass as bass
from concourse import mybir

F32 = mybir.dt.float32
F32R = mybir.dt.float32r
I32 = mybir.dt.int32
ALU = mybir.AluOpType
ACT = mybir.ActivationFunctionType
AX_X = mybir.AxisListType.X

P = 128
S = 256
D = 1024
KC = D // P
T = S // P
HG = 4
EPS = 1e-6
HGRN_CHUNK = 32
NCH = S // HGRN_CHUNK
RG_C = 8.0
SCALE = float(P) ** -0.5
NEG = -1e30
FAR = 1e6
ROUND = 1.5 * 2.0 ** 23
TWO_PI_A = 6.28125
TWO_PI_B = float(np.float32(round((2 * np.pi - TWO_PI_A) * 2.0 ** 20) / 2.0 ** 20))
TWO_PI_C = float(2 * np.pi - TWO_PI_A - TWO_PI_B)
PI_IN = 3.1415925

PARAM_ROWS = [("ev_norm", 8), ("hgrn_lb_logits", 24), ("ev_hgrn_gain", 8), ("od_norm", 8), ("od_conv_w", 32),
              ("od_conv_b", 8), ("od_rg_ba", 8), ("od_rg_bx", 8), ("od_rg_lambda", 8), ("od_ret_gain", 8),
              ("od_ret_bias", 8), ("xa_norm", 16), ("xa_mem_norm", 16)]
PARAM_AT, N_ROWS = {}, 0
for _name, _rows in PARAM_ROWS:
    PARAM_AT[_name] = N_ROWS
    N_ROWS += _rows

C_INV_RET, C_INV_MOBA, C_SIGN_RET, C_SIGN_MOBA, C_LOG_G, N_CONST = 0, 1, 2, 3, 4, 12

SLABS = []
for _g in range(2):
    SLABS += [("A", "f", "F", _g), ("A", "q", "F", _g), ("A", "i", "T", _g), ("A", "z", "F", _g)]
for _g in range(2):
    SLABS += [("B", "q", "F", _g), ("B", "k", "F", _g), ("B", "v", "T", _g), ("B", "z", "F", _g)]
SLABS += [("OUT0", (0, 0), "T", 0), ("OUT0", (0, 1), "T", 0), ("OUT0", (1, 0), "T", 0), ("OUT0", (1, 1), "T", 0)]
SLABS += [("XA0", "k", "F", 0), ("XA0", "q", "F", 0), ("XA0", "v", "T", 0), ("XA0", "o", "W", 0), ("XA1", "k", "F", 0)]
for _g in range(2):
    SLABS += [("C", "x", "F", _g), ("C", "z", "F", _g)]
for _g in range(2):
    SLABS += [("D", "q", "F", _g), ("D", "k", "F", _g), ("D", "v", "T", _g), ("D", "z", "F", _g)]
SLABS += [("OUT1", (0, 0), "T", 0), ("OUT1", (0, 1), "T", 0), ("OUT1", (1, 0), "T", 0), ("OUT1", (1, 1), "T", 0)]
SLABS += [("XA1", "v", "T", 0), ("XA1", "q", "F", 0), ("XA1", "o", "W", 0)]
NSLAB = len(SLABS)


def slab(stage, part, g=0):
    return [n for n, s in enumerate(SLABS) if s[0] == stage and s[1] == part and s[3] == g][0]


TURN = {}
_t = 0
for _n, (_stage, _part, _kind, _g) in enumerate(SLABS):
    if _stage[:3] == "OUT" and _part[0] == 1:
        TURN[_n] = TURN[_n - 2]
    else:
        TURN[_n] = _t
        _t += 2 if _kind == "W" or (_stage[:2] == "XA" and _part == "q") else 1


def hybrid_trunk(nc, I, out):
    with ExitStack() as ctx:
        def sb(name, shape, dt=F32):
            return ctx.enter_context(nc.sbuf_tensor(name, shape, dt))

        def sem(name):
            return ctx.enter_context(nc.semaphore(name))

        raw = sb("raw_weights", [P, 2, 4096])
        w_hi = sb("w_hi", [P, 4, 1024], F32R)
        w_lo = sb("w_lo", [P, 4, 1024], F32R)
        xT_hi = sb("xT_hi", [P, KC, S], F32R)
        xT_lo = sb("xT_lo", [P, KC, S], F32R)
        y_hi = sb("y_hi", [P, 2 * KC, S], F32R)
        y_lo = sb("y_lo", [P, 2 * KC, S], F32R)
        x_sb = sb("x_residual", [P, T, D])
        memT = sb("memT", [P, KC, S])
        W = sb("work", [P, 6, 1024])
        v_sb = sb("v_rows", [P, T, 512])
        zs = sb("z_silu", [P, 4, S])
        att = sb("att", [P, 4, S])
        kend_rows = sb("kend_rows", [P, T, 4, P])
        states = sb("states", [P, 4, NCH - 1, P])
        prm_rows = sb("prm_rows", [P, 2, P])
        prm = sb("prm", [P, N_ROWS])
        const = sb("const", [P, N_CONST])
        ident = sb("ident", [P, P])
        avg = sb("avg", [P, P])
        center = sb("center", [P, P])
        causal = sb("causal", [P, 3 * P])
        chunk_mask_f = sb("chunk_mask_f", [P, P])
        chunk_mask = sb("chunk_mask", [P, P], I32)
        scan_mask = sb("scan_mask", [P, 1024])
        dist = sb("dist", [P, 3 * P])
        dmask = sb("dmask", [P, 4, 3 * P])
        trig = sb("trig", [P, 4, S])
        lbp = sb("lbp", [P, 6, KC])
        soft = sb("soft", [P, 8, KC])
        st = sb("stats", [P, 64])

        def wview(i, n=1):
            return W[:, i:i + n, :].rearrange("p a b -> p (a b)")

        states_row = states[:, :, :, :].rearrange("p a b c -> p (a b c)")
        kend_row = kend_rows[:, :, :, :].rearrange("p a b c -> p (a b c)")
        mem_rows = states_row[:, 0:2048].rearrange("p (t d) -> p t d", t=T)
        rg_w = states_row[:, 0:2048].rearrange("p (m h c) -> p m h c", m=4, h=4)
        am = states_row[:, 0:1536].rearrange("p (h c) -> p h c", h=4)
        junk = kend_row
        rope_tmp = kend_row.rearrange("p (h t) -> p h t", h=4)
        fgain = wview(1)
        kx = scan_mask[:, :].rearrange("p (h t) -> p h t", h=4)

        proj = [ctx.enter_context(nc.psum_tensor(f"proj{i}", [P, 512], F32)) for i in range(4)]
        head = [ctx.enter_context(nc.psum_tensor(f"head{i}", [P, 512], F32)) for i in range(4)]

        first_landed = [sem(f"first_landed{q}") for q in range(4)]
        w_landed = [sem(f"w_landed{i}") for i in range(2)]
        hi_ready = sem("hi_ready")
        lo_ready = sem("lo_ready")
        quarter_used = sem("quarter_used")
        bank_free = [sem(f"bank_free{i}") for i in range(4)]
        x_landed = [sem(f"x_landed{t}") for t in range(T)]
        a_squared = sem("a_squared")
        mem_landed = sem("mem_landed")
        prm_landed = sem("prm_landed")
        pos_landed = sem("pos_landed")
        rg_landed = [sem(f"rg_landed{g}") for g in range(2)]
        fgain_landed = sem("fgain_landed")
        out_landed = sem("out_landed")
        masks_ready = sem("masks_ready")
        prm_turned = sem("prm_turned")
        prm_ready = sem("prm_ready")
        lb_max = sem("lb_max")
        lb_exp = sem("lb_exp")
        soft_abs = sem("soft_abs")
        soft_exp = sem("soft_exp")
        soft_ready = sem("soft_ready")
        angles_ready = sem("angles_ready")
        trig_ready = sem("trig_ready")
        sumsq = sem("sumsq")
        inv_ready = sem("inv_ready")
        rstd_ready = sem("rstd_ready")
        normed = sem("normed")
        turned = sem("turned")
        memT_ready = sem("memT_ready")
        xT_hi_ready = sem("xT_hi_ready")
        xT_lo_ready = sem("xT_lo_ready")
        mn_hi_ready = sem("mn_hi_ready")
        mn_lo_ready = sem("mn_lo_ready")
        x_added = sem("x_added")
        first_tile_filled = sem("first_tile_filled")
        z_ready = sem("z_ready")
        v_ready = sem("v_ready")
        y_ready = sem("y_ready")
        y_hi_ready = sem("y_hi_ready")
        y_lo_ready = sem("y_lo_ready")
        f_sig = sem("f_sig")
        f_ready = sem("f_ready")
        lnf_ready = sem("lnf_ready")
        b_ready = sem("b_ready")
        exps_ready = sem("exps_ready")
        bend_ready = sem("bend_ready")
        eend_ready = sem("eend_ready")
        qdec_ready = sem("qdec_ready")
        kinv_ready = sem("kinv_ready")
        kend_ready = sem("kend_ready")
        att_psum = sem("att_psum")
        att_ready = sem("att_ready")
        kend_turned = sem("kend_turned")
        kend_rows_ready = sem("kend_rows_ready")
        u_psum = sem("u_psum")
        state_ready = sem("state_ready")
        o_psum = sem("o_psum")
        o_square = sem("o_square")
        ms_psum = sem("ms_psum")
        o_rstd = sem("o_rstd")
        q_rows = sem("q_rows_copied")
        k_rows = sem("k_rows_copied")
        q_ready = sem("q_ready")
        k_ready = sem("k_ready")
        scores = sem("scores")
        row_max = sem("row_max")
        probs = sem("probs")
        probs_norm = sem("probs_norm")
        probs_turned = sem("probs_turned")
        probsT_ready = sem("probsT_ready")
        cx_ready = sem("cx_ready")
        xf_ready = sem("xf_ready")
        gates_psum = sem("gates_psum")
        rgate_ready = sem("rgate_ready")
        igate_ready = sem("igate_ready")
        decay_ready = sem("decay_ready")
        one_minus = sem("one_minus")
        root_ready = sem("root_ready")
        root_used = sem("root_used")
        h_ready = sem("h_ready")
        dmask_ready = sem("dmask_ready")
        o_copied = sem("o_copied")
        cen_psum = sem("cen_psum")
        gained = sem("gained")
        fin_ready = sem("fin_ready")
        fin_act = sem("fin_act")

        def blocks(i):
            return W[:, i, :].rearrange("p (h t) -> p h t", h=4)

        def param(name, k):
            c = PARAM_AT[name] + k
            return prm[:, c:c + 1]

        def dram_slab(n):
            stage, part, kind, g = SLABS[n]
            if stage in ("A", "B"):
                col = {"A": "qfi", "B": "qkv"}[stage].find(part) * D + 3 * D * (stage == "B")
                if part == "z":
                    col = 6 * D + D * (stage == "B")
                return I["ev_w_in"][0][:, col + 512 * g:col + 512 * g + 512].rearrange("(k p) n -> p k n", p=P)
            if stage in ("C", "D"):
                col = {"x": 0, "q": D, "k": 2 * D, "v": 3 * D, "z": 4 * D + D * (stage == "D")}[part]
                return I["od_w_in"][0][:, col + 512 * g:col + 512 * g + 512].rearrange("(k p) n -> p k n", p=P)
            if stage in ("OUT0", "OUT1"):
                w = I["ev_w_out" if stage == "OUT0" else "od_w_out"][0]
                kh, c = part
                return w[D * kh:D * kh + D, 512 * c:512 * c + 512].rearrange("(k p) n -> p k n", p=P)
            layer = int(stage[2])
            if part == "q":
                return I["xa_wq"][layer].rearrange("(k p) n -> p k n", p=P)
            if part in "kv":
                c = 512 * (part == "v")
                return I["xa_wkv"][layer][:, c:c + 512].rearrange("(k p) n -> p k n", p=P)
            return I["xa_wo"][layer].rearrange("(k p) n -> p k n", p=P)

        def raw_quarter(n, q):
            kind = SLABS[n][2]
            r = raw[:, n % 2, :]
            if kind == "F":
                return r.rearrange("p (k c) -> p k c", k=KC)[:, :, P * q:P * q + P]
            if kind == "T":
                return r.rearrange("p (k c) -> p k c", k=KC)[:, 2 * q:2 * q + 2, :]
            return r.rearrange("p (k c) -> p k c", k=4)[:, 2 * (q % 2):2 * (q % 2) + 2,
                                                        512 * (q // 2):512 * (q // 2) + 512]

        def ring_quarter(ring, n, q):
            return ring[:, q, :].rearrange("p (k c) -> p k c", k=KC if SLABS[n][2] == "F" else 2)

        def bank(n, u, half=0):
            return proj[2 * ((TURN[n] + half) % 2) + u]

        def free_of(n, u, half=0):
            return bank_free[2 * ((TURN[n] + half) % 2) + u]

        def filled(eng, n, u, half=0):
            kind = SLABS[n][2]
            eng.wait_ge(quarter_used, 4 * n + (2 * u + 2 if kind == "F" else 2 * half + 2 if kind == "W" else 4))

        def y_src(i):
            if i == 5:
                return v_sb[:, :, :].rearrange("p t c -> p (t c)").rearrange("p (h t) -> p h t", h=4)
            return blocks((4, 4, 3, 3, 2, None, 2, 2)[i])

        block = ctx.enter_context(nc.Block())

        @block.sync
        def _(sp):
            for t in range(T):
                sp.dma_start(x_sb[:, t, :], I["x"][0][P * t:P * t + P, :]).then_inc(x_landed[t], 16)
            def first_quarter(q):
                sp.dma_start(raw_quarter(0, q), dram_slab(0)[:, :, P * q:P * q + P]).then_inc(first_landed[q], 16)

            first_quarter(0)
            for name, rows in PARAM_ROWS:
                src = I[name]
                src = (src.rearrange("(k p) -> k p", p=P) if len(src.shape) == 1 else
                       src.rearrange("a (k p) -> (a k) p", p=P) if len(src.shape) == 2 else
                       src.rearrange("a b (k p) -> (a b k) p", p=P))
                r = PARAM_AT[name]
                t = r // P
                sp.dma_start(prm_rows[r - P * t:r - P * t + rows, t, :], src).then_inc(prm_landed, 16)
            for q in range(1, 4):
                first_quarter(q)
            for n in range(1, NSLAB):
                if n == 2:
                    sp.dma_start(const[:], I["shape_constants"]).then_inc(pos_landed, 16)
                    sp.dma_start(W[:, 3, 0:S].bitcast(I32), I["positions"].broadcast_to([P, S])).then_inc(pos_landed, 16)
                if n >= 2:
                    sp.wait_ge(lo_ready, 4 * (n - 1))
                if n == slab("B", "z", 0):
                    sp.dma_start(mem_rows, I["mem"][0].rearrange("(t p) d -> p t d", p=P)).then_inc(mem_landed, 16)
                if n == slab("C", "x", 0):
                    for m, name in enumerate(("od_rg_wa", "od_rg_wx")):
                        for g in range(2):
                            sp.dma_start(rg_w[:, 2 * g + m], I[name][0][4 * g:4 * g + 4].rearrange(
                                "h i j -> i h j")).then_inc(rg_landed[g], 16)
                sp.dma_start(raw[:, n % 2, :].rearrange("p (k c) -> p k c", k=4 if SLABS[n][2] == "W" else KC),
                             dram_slab(n)).then_inc(w_landed[n % 2], 16)
            sp.wait_ge(turned, 4 * 5)
            sp.dma_start(fgain, I["final_norm"].rearrange("(a d) -> a d", a=1).broadcast_to([P, D])
                         ).then_inc(fgain_landed, 16)
            for c in range(2):
                for t in range(T):
                    sp.wait_ge(fin_act if t else fin_ready, c + 1)
                    sp.dma_start(out[0][P * t:P * t + P, 512 * c:512 * c + 512], x_sb[:, t, 512 * c:512 * c + 512]
                                 ).then_inc(out_landed, 16)
            sp.wait_ge(out_landed, 16 * 4)

        @block.gpsimd
        def _(pool):
            pool.memset(ident[:], 0.0)
            pool.drain()
            pool.affine_select(out=ident[:], in_=ident[:], compare_op=ALU.not_equal, fill=1.0, base=0,
                               pattern=[[-1, P]], channel_multiplier=1).then_inc(masks_ready, 1)
            pool.memset(chunk_mask_f[:], 1.0)
            pool.memset(scan_mask[:], 1.0)
            pool.memset(att[:], 0.0)
            pool.drain()
            pool.memset(scan_mask[:].rearrange("p (c s) -> p c s", s=HGRN_CHUNK)[:, :, 0:1], 0.0)
            pool.affine_select(out=chunk_mask_f[:], in_=chunk_mask_f[:], compare_op=ALU.is_ge, fill=0.0, base=0,
                               pattern=[[1, P]], channel_multiplier=-1)
            pool.drain()
            pool.affine_select(out=chunk_mask_f[:], in_=chunk_mask_f[:], compare_op=ALU.is_ge, fill=0.0, base=0,
                               pattern=[[-HGRN_CHUNK, P // HGRN_CHUNK], [0, HGRN_CHUNK]], channel_multiplier=1)
            pool.drain()
            pool.tensor_copy(chunk_mask[:], chunk_mask_f[:]).then_inc(masks_ready, 1)
            pool.memset(avg[:], 1.0 / P)
            pool.memset(center[:], -1.0 / P)
            pool.memset(causal[:], 0.0)
            pool.iota(dist[:, 0:S], pattern=[[1, S]], base=0, channel_multiplier=-1,
                      allow_small_or_imprecise_dtypes=True)
            pool.iota(dist[:, S:3 * P], pattern=[[1, P]], base=0, channel_multiplier=-1,
                      allow_small_or_imprecise_dtypes=True)
            pool.drain()
            pool.affine_select(out=center[:], in_=center[:], compare_op=ALU.not_equal, fill=1.0 - 1.0 / P, base=0,
                               pattern=[[-1, P]], channel_multiplier=1)
            for c in (0, 2 * P):
                pool.affine_select(out=causal[:, c:c + P], in_=causal[:, c:c + P], compare_op=ALU.is_ge, fill=NEG,
                                   base=0, pattern=[[-1, P]], channel_multiplier=1)
            pool.affine_select(out=dist[:, 0:S], in_=dist[:, 0:S], compare_op=ALU.is_ge, fill=FAR, base=0,
                               pattern=[[1, S]], channel_multiplier=-1)
            pool.affine_select(out=dist[:, S:3 * P], in_=dist[:, S:3 * P], compare_op=ALU.is_ge, fill=FAR, base=0,
                               pattern=[[1, P]], channel_multiplier=-1)
            pool.drain().then_inc(masks_ready, 1)

            def y_low(i):
                G = i % 4
                pool.wait_ge(y_hi_ready, i + 1 + 2 * (i >= 4))
                pool.tensor_tensor(y_lo[:, 4 * G:4 * G + 4, :], y_src(i), y_hi[:, 4 * G:4 * G + 4, :].bitcast(F32),
                                   ALU.subtract).then_inc(y_lo_ready, 1)

            def chunk_ends(g):
                pool.wait_ge(b_ready, g + 1)
                bc = wview(2).rearrange("p (c s) -> p c s", s=HGRN_CHUNK)
                pool.tensor_tensor(wview(5).rearrange("p (c s) -> p c s", s=HGRN_CHUNK),
                                   bc[:, :, HGRN_CHUNK - 1:HGRN_CHUNK].broadcast_to([P, 4 * NCH, HGRN_CHUNK]), bc,
                                   ALU.subtract).then_inc(bend_ready, 1)
                pool.wait_ge(eend_ready, g + 1)
                pool.wait_ge(kinv_ready, g + 1)
                pool.tensor_tensor(wview(1), wview(1), wview(5), ALU.mult).then_inc(kend_ready, 1)

            def rg_products(g):
                pool.wait_ge(igate_ready, g + 1)
                xf = y_src(4 + g)
                pool.tensor_tensor(blocks(4), blocks(4), xf, ALU.mult)
                pool.wait_ge(decay_ready, g + 1)
                pool.drain()
                pool.tensor_tensor(xf, blocks(5), blocks(5), ALU.mult).then_inc(a_squared, 1)

            chunk_ends(0)
            y_low(0)
            chunk_ends(1)
            for i in range(1, 4):
                y_low(i)
            rg_products(0)
            y_low(4)
            rg_products(1)
            for i in range(5, 8):
                y_low(i)

        @block.scalar
        def _(act):
            def ahead(n, q):
                n, q = divmod(4 * n + q + 3, 4)
                if n >= NSLAB:
                    return
                if n == 0:
                    act.wait_ge(first_landed[q], 16)
                elif q == 0:
                    act.wait_ge(w_landed[n % 2], 16 * ((n + 1) // 2))
                if n >= 1:
                    act.wait_ge(quarter_used, 4 * (n - 1) + q + 1)
                act.activation(ring_quarter(w_hi, n, q), raw_quarter(n, q), ACT.Copy).then_inc(hi_ready, 1)

            def square_half(i, src, c):
                if i and c == 0:
                    act.wait_ge(inv_ready, i)
                for t in range(T):
                    act.drain()
                    last = act.activation(junk[:, 0:512], src[:, t, 512 * c:512 * c + 512], ACT.Square,
                                          accum_out=st[:, 2 * c + t:2 * c + t + 1])
                last.then_inc(sumsq, 1)

            def root(i):
                act.wait_ge(inv_ready, i + 1)
                act.activation(st[:, 6:8], st[:, 4:6], ACT.Sqrt).then_inc(rstd_ready, 1)

            def xT_high(i, j0, gain, gk):
                for k in range(KC):
                    if k % 2 == 0:
                        act.wait_ge(turned, j0 + k // 2 + 1)
                    act.activation(xT_hi[:, k, :], head[k // 2][:, S * (k % 2):S * (k % 2) + S], ACT.Copy,
                                   scale=param(gain, gk + k)).then_inc(xT_hi_ready, 1)

            def mn_high(layer):
                for k in range(KC):
                    act.activation(y_hi[:, k, :], memT[:, k, :], ACT.Copy,
                                   scale=param("xa_mem_norm", KC * layer + k)).then_inc(mn_hi_ready, 1)

            def silu(n):
                i = {"A": 0, "B": 2, "C": 4, "D": 6}[SLABS[n][0]] + SLABS[n][3]
                filled(act, n, 1)
                if i:
                    act.wait_ge(y_ready, i)
                for u in range(2):
                    act.activation(zs[:, 2 * u:2 * u + 2, :], bank(n, u)[:].rearrange("p (h t) -> p h t", h=2),
                                   ACT.Silu).then_inc(z_ready, 1)
                act.drain().then_inc(free_of(n, 0), 1)
                act.nop().then_inc(free_of(n, 1), 1)

            def copy_bank(n, u, dst, s):
                filled(act, n, u)
                act.activation(dst, bank(n, u)[:], ACT.Copy).then_inc(s, 1)
                act.drain().then_inc(free_of(n, u), 1)

            def v_rows(n):
                for t in range(T):
                    copy_bank(n, t, v_sb[:, t, :], v_ready)

            def y_high(i):
                G = i % 4
                act.wait_ge(y_ready, i + 1)
                act.activation(y_hi[:, 4 * G:4 * G + 4, :], y_src(i), ACT.Copy).then_inc(y_hi_ready, 1)

            act.preload_act_table(ACT.Sqrt)
            for t in range(T):
                act.wait_ge(x_landed[t], 16)
                act.drain()
                act.activation(junk[:], x_sb[:, t, :], ACT.Square, accum_out=st[:, t:t + 1]).then_inc(sumsq, 1)
            root(0)
            ahead(-1, 1)
            act.wait_ge(prm_turned, 1)
            act.activation(prm[:], proj[0][:, 0:N_ROWS], ACT.Copy).then_inc(prm_ready, 1)
            act.drain()
            xT_high(0, 0, "ev_norm", 0)
            ahead(-1, 2)
            ahead(-1, 3)
            act.wait_ge(lb_max, 1)
            act.activation(lbp[:, 0:3, :], lbp[:, 0:3, :], ACT.Exp).then_inc(lb_exp, 1)
            act.wait_ge(soft_abs, 1)
            act.activation(soft[:, 2, :], soft[:, 1, :], ACT.Exp, scale=-1.0).then_inc(soft_exp, 1)

            def squares_a(g):
                for u in range(2):
                    act.wait_ge(o_psum, 2 * g + u + 1)
                    act.activation(W[:, 5, 512 * u:512 * u + 512], head[u][:], ACT.Square).then_inc(o_square, 1)

            def rstd_a(g):
                for u in range(2):
                    act.wait_ge(ms_psum, 2 * g + u + 1)
                    act.activation(W[:, 5, 512 * u:512 * u + 512], head[2 + u][:], ACT.Ln, bias=st[:, 60:61])
                act.drain()
                act.activation(wview(5), wview(5), ACT.Exp, scale=-0.5).then_inc(o_rstd, 1)

            def stage_a(g):
                f, q, i, z = (slab("A", c, g) for c in "fqiz")
                ahead(f, 0)
                if g:
                    silu(slab("A", "z", 0))
                ahead(f, 1)
                ahead(f, 2)
                filled(act, f, 0)
                act.activation(W[:, 0, 0:512], bank(f, 0)[:], ACT.Sigmoid).then_inc(f_sig, 1)
                act.drain().then_inc(free_of(f, 0), 1)
                ahead(f, 3)
                if g:
                    squares_a(0)
                ahead(q, 0)
                filled(act, f, 1)
                act.activation(W[:, 0, 512:1024], bank(f, 1)[:], ACT.Sigmoid).then_inc(f_sig, 1)
                act.drain().then_inc(free_of(f, 1), 1)
                if g == 0:
                    act.wait_ge(angles_ready, 1)
                    act.activation(trig[:], trig[:], ACT.Sin).then_inc(trig_ready, 1)
                act.preload_act_table_set("natural_log_exp_and_others")
                ahead(q, 1)
                if g:
                    rstd_a(0)
                ahead(q, 2)
                act.wait_ge(f_ready, g + 1)
                act.activation(wview(0), wview(0), ACT.Ln).then_inc(lnf_ready, 1)
                ahead(q, 3)
                if g:
                    y_high(0)
                ahead(i, 0)
                act.wait_ge(b_ready, g + 1)
                act.activation(wview(3), wview(2), ACT.Exp).then_inc(exps_ready, 1)
                act.activation(wview(0), wview(2), ACT.Exp, scale=-1.0).then_inc(exps_ready, 1)
                ahead(i, 1)
                act.wait_ge(bend_ready, g + 1)
                act.activation(wview(5), wview(5), ACT.Exp).then_inc(eend_ready, 1)
                ahead(i, 2)
                ahead(i, 3)
                ahead(z, 0)
                v_rows(i)
                for u in range(2):
                    act.wait_ge(kend_turned, 2 * g + u + 1)
                    act.activation(kend_rows[:, u, :, :].rearrange("p h d -> p (h d)"), head[2 + u][:], ACT.Copy
                                   ).then_inc(kend_rows_ready, 1)
                ahead(z, 1)
                ahead(z, 2)
                ahead(z, 3)

            def softmax_exp(i, h, moba):
                act.wait_ge(row_max, i)
                for t in range(T):
                    if moba:
                        pr = wview(2, 2)[:, 384 * h + 128 * t:384 * h + 128 + 256 * t]
                    else:
                        pr = wview(2, 2)[:, 512 * h + 256 * t:512 * h + 256 * t + 256]
                    c = 2 * h + t
                    src = pr if moba else head[h][:, 256 * t:256 * t + 256]
                    act.activation(pr, src, ACT.Exp, bias=st[:, 24 + c:25 + c], scale=SCALE,
                                   accum_out=st[:, 32 + c:33 + c]).then_inc(probs, 1)

            def stage_b(g):
                q, k, v, z = (slab("B", c, g) for c in "qkvz")
                ahead(q, 0)
                silu(slab("A", "z", 1) if g == 0 else slab("B", "z", 0))
                ahead(q, 1)
                ahead(q, 2)
                copy_bank(q, 0, W[:, 0, 0:512], q_rows)
                ahead(q, 3)
                if g:
                    y_high(2)
                else:
                    squares_a(1)
                ahead(k, 0)
                copy_bank(q, 1, W[:, 0, 512:1024], q_rows)
                ahead(k, 1)
                if g == 0:
                    act.preload_act_table_set("natural_log_exp_and_others")
                    rstd_a(1)
                else:
                    act.wait_ge(mem_landed, 16)
                    square_half(1, mem_rows, 0)
                    square_half(1, mem_rows, 1)
                ahead(k, 2)
                copy_bank(k, 0, W[:, 1, 0:512], k_rows)
                if g:
                    act.preload_act_table(ACT.Sqrt)
                    root(1)
                ahead(k, 3)
                if g == 0:
                    y_high(1)
                ahead(v, 0)
                copy_bank(k, 1, W[:, 1, 512:1024], k_rows)
                ahead(v, 1)
                ahead(v, 2)
                if g:
                    for j in range(4):
                        act.wait_ge(turned, 4 + j + 1)
                        act.activation(memT[:, 2 * j:2 * j + 2, :], head[j][:].rearrange("p (k t) -> p k t", k=2),
                                       ACT.Copy).then_inc(memT_ready, 1)
                ahead(v, 3)
                ahead(z, 0)
                v_rows(v)
                softmax_exp(8 * g + 2, 0, True)
                ahead(z, 1)
                softmax_exp(8 * g + 4, 1, True)
                ahead(z, 2)
                softmax_exp(8 * g + 6, 2, True)
                softmax_exp(8 * g + 8, 3, True)
                ahead(z, 3)

            def turned_probs(i, h, cols):
                act.wait_ge(probs_turned, i)
                act.activation(wview(4, 2)[:, cols * h:cols * h + cols], head[h][:, 0:cols], ACT.Copy
                               ).then_inc(probsT_ready, 1)

            def cross(layer):
                X = f"XA{layer}"
                nk, nq, nv, no = (slab(X, c) for c in "kqvo")
                base = 16 + 8 * layer
                first = nk if layer == 0 else nv
                ahead(first, 0)
                norm_high(2 + 2 * layer)
                ahead(first, 1)
                if layer == 0:
                    ahead(first, 2)
                    copy_bank(nk, 0, kx[:, 0:2, :].rearrange("p h t -> p (h t)"), k_rows)
                    ahead(first, 3)
                else:
                    ahead(first, 2)
                    ahead(first, 3)
                xT_high(1 + 2 * layer, 8 + 8 * layer, "xa_norm", KC * layer)
                ahead(nq, 0)
                if layer == 0:
                    copy_bank(nk, 1, kx[:, 2:4, :].rearrange("p h t -> p (h t)"), k_rows)
                else:
                    v_rows(nv)
                act.preload_act_table(ACT.Exp)

                def query(h):
                    act.wait_ge(quarter_used, 4 * nq + h + 1)
                    act.activation(blocks(0)[:, h, :], bank(nq, h % 2, h // 2)[:, 0:S], ACT.Copy).then_inc(q_rows, 1)
                    act.drain().then_inc(free_of(nq, h % 2, h // 2), 1)

                for h in range(4):
                    if h < 3:
                        ahead(nq, h + 1)
                    query(h)
                    if h >= 2:
                        softmax_exp(base + 2 * h - 2, h - 2, False)
                nxt = nq + 1
                if layer == 0:
                    ahead(nxt, 0)
                softmax_exp(base + 6, 2, False)
                if layer == 0:
                    ahead(nxt, 1)
                softmax_exp(base + 8, 3, False)
                if layer == 0:
                    ahead(nxt, 2)
                    turned_probs(8 + 1, 0, 512)
                    turned_probs(8 + 2, 1, 512)
                    ahead(nxt, 3)
                    v_rows(nv)
                    turned_probs(8 + 3, 2, 512)
                    turned_probs(8 + 4, 3, 512)
                else:
                    for h in range(4):
                        turned_probs(12 + h + 1, h, 512)
                    ahead(nxt, 0)
                for u in range(2):
                    act.wait_ge(o_psum, 8 + 2 * layer + (4 if layer else 0) + u + 1)
                    act.activation(y_hi[:, KC + 2 * u:KC + 2 * u + 2, :], head[u][:].rearrange("p (h t) -> p h t", h=2),
                                   ACT.Copy).then_inc(y_hi_ready, 1)

            def norm_high(i):
                act.preload_act_table(ACT.Sqrt)
                act.wait_ge(x_added, 4 * (i - 1))
                square_half(i, x_sb, 1)
                root(i)

            def out_stage(name, layer, i):
                n = slab(name, (0, 0))
                ahead(n, 0)
                silu(slab("B" if layer == 0 else "D", "z", 1))
                ahead(n, 1)
                if layer == 0:
                    for h in range(4):
                        turned_probs(4 + h + 1, h, 384)
                else:
                    rstd_d(1)
                ahead(n, 2)
                if layer:
                    y_high(7)
                ahead(n, 3)
                ahead(n + 1, 0)
                if layer == 0:
                    y_high(3)
                for q in range(1, 4):
                    ahead(n + 1, q)
                ahead(n + 2, 0)
                mn_high(layer)
                for q in range(1, 4):
                    ahead(n + 2, q)
                ahead(n + 3, 0)
                ahead(n + 3, 1)
                act.wait_ge(x_added, 4 * (i - 1) - 2)
                square_half(i, x_sb, 0)
                ahead(n + 3, 2)
                ahead(n + 3, 3)

            def wo_stage(no, i):
                for q in range(4):
                    ahead(no, q)
                    if q == 1:
                        mn_high(1)
                    if q == 3:
                        act.wait_ge(x_added, 4 * (i - 1) - 2)
                        square_half(i, x_sb, 0)

            stage_a(0)
            stage_a(1)
            stage_b(0)
            for h in range(4):
                turned_probs(h + 1, h, 384)
            stage_b(1)
            out_stage("OUT0", 0, 2)
            cross(0)
            wo_stage(slab("XA0", "o"), 3)
            n = slab("XA1", "k")
            ahead(n, 0)
            norm_high(3)
            ahead(n, 1)
            ahead(n, 2)
            copy_bank(n, 0, kx[:, 0:2, :].rearrange("p h t -> p (h t)"), k_rows)
            ahead(n, 3)
            xT_high(2, 12, "od_norm", 0)

            def silu_of_c(g):
                silu(slab("C", "z", g))

            def gate(g, m):
                name, s = (("od_rg_ba", rgate_ready), ("od_rg_bx", igate_ready))[m]
                if g:
                    act.wait_ge(h_ready if m else root_used, g)
                for h in range(4):
                    if h % 2 == 0:
                        act.wait_ge(gates_psum, 4 * g + 2 * m + h // 2 + 1)
                    last = act.activation(blocks(3 + m)[:, h, :], head[2 * m + h // 2][:, S * (h % 2):S * (h % 2) + S],
                                          ACT.Sigmoid, bias=param(name, 4 * g + h))
                last.then_inc(s, 1)

            def decays(g):
                act.preload_act_table(ACT.Exp)
                act.drain()
                act.wait_ge(soft_ready, 1)
                for h in range(4):
                    act.activation(blocks(5)[:, h, :], blocks(3)[:, h, :], ACT.Exp,
                                   scale=soft[:, 7, 4 * g + h:4 * g + h + 1])

            def tanhs(g):
                act.drain()
                for h in range(4):
                    last = act.activation(blocks(3)[:, h, :], blocks(3)[:, h, :], ACT.Tanh,
                                          scale=soft[:, 6, 4 * g + h:4 * g + h + 1])
                last.then_inc(decay_ready, 1)

            def root_c(g):
                act.wait_ge(one_minus, g + 1)
                act.activation(wview(3), wview(3), ACT.Sqrt).then_inc(root_ready, 1)

            def stage_c(g):
                cx, z = slab("C", "x", g), slab("C", "z", g)
                cxp = wview(0, 2)[:, 0:4 * (S + 3)].rearrange("p (h t) -> p h t", h=4)

                def rows(u):
                    filled(act, cx, u)
                    if g:
                        act.wait_ge(xf_ready, 2 * g)
                    act.activation(cxp[:, 2 * u:2 * u + 2, 3:S + 3], bank(cx, u)[:].rearrange("p (h t) -> p h t", h=2),
                                   ACT.Copy).then_inc(cx_ready, 1)
                    act.drain().then_inc(free_of(cx, u), 1)

                ahead(cx, 0)
                if g:
                    gate(0, 1)
                    silu_of_c(0)
                else:
                    n = slab("XA1", "k")
                    copy_bank(n, 1, kx[:, 2:4, :].rearrange("p h t -> p (h t)"), k_rows)
                ahead(cx, 1)
                if g:
                    decays(0)
                ahead(cx, 2)
                rows(0)
                ahead(cx, 3)
                rows(1)
                if g:
                    tanhs(0)
                ahead(z, 0)
                ahead(z, 1)
                ahead(z, 2)
                if g:
                    root_c(0)
                ahead(z, 3)
                gate(g, 0)

            def rstd_d(g):
                for u in range(2):
                    act.wait_ge(ms_psum, 4 + 2 * g + u + 1)
                    act.activation(W[:, 4, 512 * u:512 * u + 512], head[u][:], ACT.Ln, bias=st[:, 60:61])
                act.drain()
                act.activation(wview(4), wview(4), ACT.Exp, scale=-0.5).then_inc(o_rstd, 1)

            def dm(g, h):
                i = 4 * g + h
                if g:
                    act.wait_ge(att_ready, 8 + i - 3)
                act.activation(dmask[:, h, :], dist[:], ACT.Exp, scale=const[:, C_LOG_G + i:C_LOG_G + i + 1],
                               bias=st[:, 61:62]).then_inc(dmask_ready, 1)

            def stage_d(g):
                q, k, v, z = (slab("D", c, g) for c in "qkvz")
                ahead(q, 0)
                if g == 0:
                    gate(1, 1)
                else:
                    rstd_d(0)
                ahead(q, 1)
                if g == 0:
                    y_high(4)
                    silu_of_c(1)
                else:
                    silu(slab("D", "z", 0))
                ahead(q, 2)
                if g == 0:
                    decays(1)
                ahead(q, 3)
                if g == 0:
                    tanhs(1)
                ahead(k, 0)
                if g:
                    y_high(6)
                ahead(k, 1)
                for h in range(4):
                    dm(g, h)
                    if h == 1:
                        ahead(k, 2)
                    if h == 3:
                        ahead(k, 3)
                ahead(v, 0)
                if g == 0:
                    root_c(1)
                ahead(v, 1)
                ahead(v, 2)
                ahead(v, 3)
                if g == 0:
                    y_high(5)
                ahead(z, 0)
                if g == 0:
                    act.wait_ge(y_lo_ready, 8)
                v_rows(v)
                ahead(z, 1)
                ahead(z, 2)
                for u in range(2):
                    act.wait_ge(o_psum, 10 + 2 * g + u + 1)
                    act.activation(W[:, 4, 512 * u:512 * u + 512], head[u][:], ACT.Copy).then_inc(o_copied, 1)
                ahead(z, 3)
                for u in range(2):
                    act.wait_ge(cen_psum, 2 * g + u + 1)
                    act.activation(W[:, 5, 512 * u:512 * u + 512], head[2 + u][:], ACT.Square).then_inc(o_square, 1)
                act.preload_act_table_set("natural_log_exp_and_others")

            stage_c(0)
            stage_c(1)
            stage_d(0)
            stage_d(1)
            out_stage("OUT1", 1, 4)
            cross(1)
            act.preload_act_table(ACT.Sqrt)
            act.wait_ge(x_added, 14)
            square_half(5, x_sb, 0)
            for t in range(T):
                act.wait_ge(x_added, 15 + t)
                act.drain()
                last = act.activation(junk[:, 0:512], x_sb[:, t, 512:1024], ACT.Square,
                                      accum_out=st[:, 2 + t:3 + t])
            last.then_inc(sumsq, 1)
            root(5)
            act.wait_ge(gained, 2)
            act.drain()
            for c in range(2):
                act.activation(x_sb[:, 1, 512 * c:512 * c + 512], W[:, 3, 512 * c:512 * c + 512], ACT.Copy,
                               scale=st[:, 7:8]).then_inc(fin_act, 1)

        @block.vector
        def _(dve):
            def ahead(n, q):
                n, q = divmod(4 * n + q + 3, 4)
                if n >= NSLAB:
                    return
                dve.wait_ge(hi_ready, 4 * n + q + 1)
                dve.tensor_tensor(ring_quarter(w_lo, n, q), raw_quarter(n, q),
                                  ring_quarter(w_hi, n, q).bitcast(F32), ALU.subtract).then_inc(lo_ready, 1)

            def rstd(i):
                dve.wait_ge(sumsq, 2 * (i + 1))
                dve.tensor_tensor(st[:, 4:6], st[:, 0:2], st[:, 2:4], ALU.add)
                dve.drain()
                dve.tensor_scalar(st[:, 4:6], st[:, 4:6], 1.0 / D, EPS, ALU.mult, ALU.add)
                dve.drain()
                dve.reciprocal(st[:, 4:6], st[:, 4:6]).then_inc(inv_ready, 1)
                dve.wait_ge(rstd_ready, i + 1)

            def norm_rows(i, src, dst):
                rstd(i)
                for c in range(2):
                    for t in range(T):
                        last = dve.tensor_scalar(dst[:, t, 512 * c:512 * c + 512], src[:, t, 512 * c:512 * c + 512],
                                                 st[:, 6 + t:7 + t], None, ALU.mult)
                    last.then_inc(normed, 1)

            def xT_low(i, gain, gk):
                for k in range(KC):
                    dve.wait_ge(xT_hi_ready, KC * i + k - k % 2 + 2)
                    dve.scalar_tensor_tensor(out=xT_lo[:, k, :], in0=head[k // 2][:, S * (k % 2):S * (k % 2) + S],
                                             scalar=param(gain, gk + k), in1=xT_hi[:, k, :].bitcast(F32),
                                             op0=ALU.mult, op1=ALU.subtract).then_inc(xT_lo_ready, 1)

            def mn_low(layer, use, ks):
                for k in ks:
                    dve.wait_ge(mn_hi_ready, KC * use + k + 1)
                    dve.scalar_tensor_tensor(out=y_lo[:, k, :], in0=memT[:, k, :],
                                             scalar=param("xa_mem_norm", KC * layer + k),
                                             in1=y_hi[:, k, :].bitcast(F32),
                                             op0=ALU.mult, op1=ALU.subtract).then_inc(mn_lo_ready, 1)

            def add_turn(n, c, half=0):
                for t in range(T):
                    if t == 0 and n == NSLAB - 1 and half == 1:
                        dve.wait_ge(first_tile_filled, 1)
                    else:
                        filled(dve, n, t, half)
                    dve.tensor_tensor(x_sb[:, t, 512 * c:512 * c + 512], bank(n, t, half)[:],
                                      x_sb[:, t, 512 * c:512 * c + 512], ALU.add).then_inc(x_added, 1)
                dve.drain().then_inc(free_of(n, 0, half), 1)
                dve.nop().then_inc(free_of(n, 1, half), 1)

            dve.memset(st[:, 60:61], EPS)
            dve.memset(st[:, 61:62], float(np.log(SCALE)))
            dve.memset(st[:, 2:4], 0.0)
            dve.drain()
            norm_rows(0, x_sb, W[:, 0:2, :])
            ahead(-1, 1)
            dve.wait_ge(prm_ready, 1)
            xT_low(0, "ev_norm", 0)
            ahead(-1, 2)
            ahead(-1, 3)
            lg = prm[:, PARAM_AT["hgrn_lb_logits"]:PARAM_AT["hgrn_lb_logits"] + 3 * KC].rearrange(
                "p (j k) -> p j k", j=3)
            dve.tensor_tensor(lbp[:, 3, :], lg[:, 0, :], lg[:, 1, :], ALU.max)
            dve.drain()
            dve.tensor_tensor(lbp[:, 3, :], lbp[:, 3, :], lg[:, 2, :], ALU.max)
            dve.drain()
            for j in range(3):
                last = dve.tensor_tensor(lbp[:, j, :], lg[:, j, :], lbp[:, 3, :], ALU.subtract)
            last.then_inc(lb_max, 1)
            lam = prm[:, PARAM_AT["od_rg_lambda"]:PARAM_AT["od_rg_lambda"] + KC]
            dve.tensor_scalar(soft[:, 0, :], lam, -1.0, None, ALU.mult)
            dve.drain()
            dve.tensor_tensor(soft[:, 1, :], lam, soft[:, 0, :], ALU.max).then_inc(soft_abs, 1)
            dve.wait_ge(lb_exp, 1)
            dve.tensor_tensor(lbp[:, 3, :], lbp[:, 0, :], lbp[:, 1, :], ALU.add)
            dve.drain()
            dve.tensor_tensor(lbp[:, 3, :], lbp[:, 3, :], lbp[:, 2, :], ALU.add)
            dve.drain()
            dve.reciprocal(lbp[:, 3, :], lbp[:, 3, :])
            dve.drain()
            dve.tensor_tensor(lbp[:, 4, :], lbp[:, 0, :], lbp[:, 3, :], ALU.mult)
            dve.drain()
            dve.tensor_scalar(lbp[:, 5, :], lbp[:, 4, :], -1.0, 1.0, ALU.mult, ALU.add)

            def angles():
                pos = W[:, 3, S:2 * S]
                ang = trig
                kk = wview(4).rearrange("p (a t) -> p a t", a=4)[:, 0:2, :]
                dve.wait_ge(pos_landed, 32)
                dve.tensor_copy(pos, W[:, 3, 0:S].bitcast(I32))
                dve.drain()
                for j, c in enumerate((C_INV_RET, C_INV_MOBA)):
                    dve.tensor_scalar(ang[:, 2 * j + 1, :], pos, const[:, c:c + 1], None, ALU.mult)
                dve.drain()
                sn = ang[:, 1:4:2, :]
                cs = ang[:, 0:3:2, :]
                dve.tensor_scalar(kk, sn, float(1 / (2 * np.pi)), ROUND, ALU.mult, ALU.add)
                dve.drain()
                dve.tensor_scalar(kk, kk, ROUND, None, ALU.subtract)
                dve.drain()
                ahead(slab("A", "f", 0), 2)
                for c in (TWO_PI_A, TWO_PI_B, TWO_PI_C):
                    dve.scalar_tensor_tensor(out=sn, in0=kk, scalar=-c, in1=sn, op0=ALU.mult, op1=ALU.add)
                    dve.drain()
                ahead(slab("A", "f", 0), 3)
                dve.tensor_scalar(cs, sn, float(np.pi / 2), None, ALU.add)
                dve.drain()
                dve.tensor_scalar(kk, cs, float(np.pi), -2 * float(np.pi), ALU.is_gt, ALU.mult)
                dve.drain()
                dve.tensor_tensor(cs, cs, kk, ALU.add)
                dve.drain()
                dve.tensor_scalar(trig[:], trig[:], PI_IN, -PI_IN, ALU.min, ALU.max).then_inc(angles_ready, 1)

            def softplus():
                dve.wait_ge(soft_exp, 1)
                e, s, s2, p = (soft[:, j, :] for j in (2, 3, 4, 5))
                dve.tensor_scalar(s, e, 2.0, None, ALU.add)
                dve.drain()
                dve.reciprocal(s, s)
                dve.drain()
                dve.tensor_tensor(s, s, e, ALU.mult)
                dve.drain()
                dve.tensor_tensor(s2, s, s, ALU.mult)
                dve.drain()
                dve.tensor_scalar(p, s2, 1.0 / 15, None, ALU.mult)
                dve.drain()
                for c in (13, 11, 9, 7, 5, 3):
                    dve.scalar_tensor_tensor(out=p, in0=p, scalar=1.0 / c, in1=s2, op0=ALU.add, op1=ALU.mult)
                    dve.drain()
                dve.scalar_tensor_tensor(out=p, in0=p, scalar=1.0, in1=s, op0=ALU.add, op1=ALU.mult)
                dve.tensor_scalar(soft[:, 0, :], soft[:, 0, :], 0.0, None, ALU.max)
                dve.drain()
                dve.scalar_tensor_tensor(out=p, in0=p, scalar=2.0, in1=soft[:, 0, :], op0=ALU.mult, op1=ALU.add)
                dve.drain()
                dve.tensor_scalar(soft[:, 6, :], p, RG_C, None, ALU.mult)
                dve.tensor_scalar(soft[:, 7, :], p, -RG_C, None, ALU.mult).then_inc(soft_ready, 1)

            def sign_trig():
                dve.wait_ge(trig_ready, 1)
                dve.tensor_scalar(trig[:, 1, :], trig[:, 1, :], const[:, C_SIGN_RET:C_SIGN_RET + 1], None, ALU.mult)
                dve.tensor_scalar(trig[:, 3, :], trig[:, 3, :], const[:, C_SIGN_MOBA:C_SIGN_MOBA + 1], None, ALU.mult)

            def forget(g, u):
                dve.wait_ge(f_sig, 2 * g + u + 1)
                for h in (2 * u, 2 * u + 1):
                    dve.tensor_scalar(blocks(0)[:, h, :], blocks(0)[:, h, :], lbp[:, 5, 4 * g + h:4 * g + h + 1],
                                      lbp[:, 4, 4 * g + h:4 * g + h + 1], ALU.mult, ALU.add)

            def chain(g, h):
                for c in range(NCH - 1):
                    u = head[c % 4][:, P * (2 * (h % 2) + c // 4):P * (2 * (h % 2) + c // 4) + P]
                    if c == 0:
                        last = dve.tensor_copy(states[:, h, 0, :], u)
                    else:
                        col = S * h + HGRN_CHUNK * c + HGRN_CHUNK - 1
                        dve.drain()
                        last = dve.scalar_tensor_tensor(out=states[:, h, c, :], in0=states[:, h, c - 1, :],
                                                        scalar=W[:, 3, col:col + 1], in1=u, op0=ALU.mult,
                                                        op1=ALU.add)
                last.then_inc(state_ready, 1)

            def gated_a(g):
                dve.wait_ge(o_rstd, g + 1)
                dve.wait_ge(z_ready, 2 * (g + 1))
                for h in range(4):
                    dve.scalar_tensor_tensor(out=blocks(4)[:, h, :], in0=head[h // 2][:, S * (h % 2):S * (h % 2) + S],
                                             scalar=param("ev_hgrn_gain", 4 * g + h), in1=blocks(5)[:, h, :],
                                             op0=ALU.mult, op1=ALU.mult)
                dve.drain()
                dve.tensor_tensor(blocks(4), blocks(4), zs[:], ALU.mult).then_inc(y_ready, 1)

            def stage_a(g):
                f, q, i, z = (slab("A", c, g) for c in "fqiz")
                ahead(f, 0)
                if g:
                    chain(0, 3)
                ahead(f, 1)
                if g:
                    ahead(f, 2)
                    ahead(f, 3)
                else:
                    angles()
                forget(g, 0)
                ahead(q, 0)
                forget(g, 1)
                dve.drain()
                dve.tensor_scalar(wview(1), wview(0), -1.0, 1.0, ALU.mult, ALU.add).then_inc(f_ready, 1)
                ahead(q, 1)
                if g:
                    gated_a(0)
                else:
                    sign_trig()
                ahead(q, 2)
                ahead(q, 3)
                dve.wait_ge(lnf_ready, g + 1)
                if g == 0:
                    dve.wait_ge(masks_ready, 2)
                dve.tensor_tensor_scan(wview(2), scan_mask[:], wview(0), 0.0, ALU.mult, ALU.add).then_inc(b_ready, 1)
                ahead(i, 0)
                ahead(i, 1)
                dve.wait_ge(exps_ready, 2 * g + 2)
                dve.tensor_tensor(wview(0), wview(1), wview(0), ALU.mult).then_inc(kinv_ready, 1)
                if g:
                    dve.wait_ge(y_lo_ready, g)
                for u in range(2):
                    filled(dve, q, u)
                    dve.tensor_tensor(W[:, 4, 512 * u:512 * u + 512], bank(q, u)[:], W[:, 3, 512 * u:512 * u + 512],
                                      ALU.mult).then_inc(qdec_ready, 1)
                dve.drain().then_inc(free_of(q, 0), 1)
                dve.nop().then_inc(free_of(q, 1), 1)
                ahead(i, 2)
                ahead(i, 3)
                ahead(z, 0)
                for h in range(4):
                    dve.wait_ge(att_psum, 2 * g + h // 2 + 1)
                    for t in range(T):
                        c = S * (h % 2) + P * t
                        last = dve.copy_predicated(att[:, h, P * t:P * t + P], chunk_mask[:],
                                                   head[h // 2][:, c:c + P])
                    last.then_inc(att_ready, 1)
                ahead(z, 1)
                ahead(z, 2)
                dve.wait_ge(u_psum, 2 * g + 1)
                chain(g, 0)
                chain(g, 1)
                ahead(z, 3)
                dve.wait_ge(u_psum, 2 * g + 2)
                chain(g, 2)

            def rope_moba(w, ready, done, cnt, n, q):
                dve.wait_ge(ready, cnt)
                mask = [(j + 16) % 32 for j in range(32)]
                x32 = blocks(w)[0:32, :, :]
                t32 = blocks(2)[0:32, :, :]
                cos = trig[0:32, 2:3, :].broadcast_to([32, 4, S])
                sin = trig[0:32, 3:4, :].broadcast_to([32, 4, S])
                dve.drain()
                dve.stream_shuffle(W[0:32, 2, :], W[0:32, w, :], mask)
                dve.drain()
                ahead(n, q)
                dve.tensor_tensor(t32, t32, sin, ALU.mult)
                dve.tensor_tensor(x32, x32, cos, ALU.mult)
                dve.drain()
                dve.tensor_tensor(x32, x32, t32, ALU.add).then_inc(done, 1)

            def softmax_max(i, h, moba):
                dve.wait_ge(scores, i)
                if moba:
                    for t in range(T):
                        c = 2 * h + t
                        a, b = 128 * t, 128 + 256 * t
                        sc = wview(2, 2)[:, 384 * h + a:384 * h + b]
                        dve.tensor_tensor_reduce(out=sc, in0=head[h][:, a:b], in1=causal[:, a:b], scale=1.0,
                                                 scalar=3 * NEG, op0=ALU.add, op1=ALU.max,
                                                 accum_out=st[:, 16 + c:17 + c])
                else:
                    dve.tensor_reduce(st[:, 16 + 2 * h:18 + 2 * h], head[h][:].rearrange("p (t k) -> p t k", t=2),
                                      AX_X, ALU.max)
                dve.drain()
                dve.tensor_scalar(st[:, 24 + 2 * h:26 + 2 * h], st[:, 16 + 2 * h:18 + 2 * h], -SCALE, None, ALU.mult
                                  ).then_inc(row_max, 2)

            def softmax_norm(i, h, moba):
                dve.wait_ge(probs, i)
                dve.reciprocal(st[:, 40 + 2 * h:42 + 2 * h], st[:, 32 + 2 * h:34 + 2 * h])
                dve.drain()
                for t in range(T):
                    c = 40 + 2 * h + t
                    pr = (wview(2, 2)[:, 384 * h + 128 * t:384 * h + 128 + 256 * t] if moba else
                          wview(2, 2)[:, 512 * h + 256 * t:512 * h + 256 * t + 256])
                    last = dve.tensor_scalar(pr, pr, st[:, c:c + 1], None, ALU.mult)
                last.then_inc(probs_norm, 1)

            def gated_b(g):
                dve.wait_ge(z_ready, 2 * (3 + g))
                for u in range(2):
                    dve.wait_ge(o_psum, 4 + 2 * g + u + 1)
                    last = dve.tensor_tensor(W[:, 3, 512 * u:512 * u + 512], head[u][:],
                                             zs[:, 2 * u:2 * u + 2, :].rearrange("p h t -> p (h t)"), ALU.mult)
                last.then_inc(y_ready, 1)

            def stage_b(g):
                q, k, v, z = (slab("B", c, g) for c in "qkvz")
                ahead(q, 0)
                if g == 0:
                    chain(1, 3)
                ahead(q, 1)
                ahead(q, 2)
                ahead(q, 3)
                if g:
                    gated_b(0)
                ahead(k, 0)
                ahead(k, 1)
                if g == 0:
                    gated_a(1)
                ahead(k, 2)
                if g:
                    norm_rows(1, mem_rows, mem_rows)
                rope_moba(0, q_rows, q_ready, 2 * g + 2, k, 3)
                ahead(v, 0)
                rope_moba(1, k_rows, k_ready, 2 * g + 2, v, 1)
                ahead(v, 2)
                ahead(v, 3)
                ahead(z, 0)
                if g == 0:
                    softplus()
                dve.wait_ge(y_lo_ready, 2 + g)
                if g == 0:
                    dve.wait_ge(masks_ready, 3)
                softmax_max(4 * g + 1, 0, True)
                softmax_max(4 * g + 2, 1, True)
                ahead(z, 1)
                softmax_max(4 * g + 3, 2, True)
                softmax_max(4 * g + 4, 3, True)
                ahead(z, 2)
                softmax_norm(8 * g + 2, 0, True)
                softmax_norm(8 * g + 4, 1, True)
                softmax_norm(8 * g + 6, 2, True)
                ahead(z, 3)
                softmax_norm(8 * g + 8, 3, True)

            def cross(layer):
                X = f"XA{layer}"
                nk, nq, nv, no = (slab(X, c) for c in "kqvo")
                base = 16 + 8 * layer
                first = nk if layer == 0 else nv
                add_turn(first - 1, 1)
                ahead(first, 0)
                norm_rows(2 + 2 * layer, x_sb, W[:, 0:2, :])
                for q in range(1, 4):
                    ahead(first, q)
                xT_low(1 + 2 * layer, "xa_norm", KC * layer)
                ahead(nq, 0)
                ahead(nq, 1)
                ahead(nq, 2)
                softmax_max(8 + 4 * layer + 1, 0, False)
                ahead(nq, 3)
                softmax_max(8 + 4 * layer + 2, 1, False)
                softmax_norm(base + 2, 0, False)
                if layer == 0:
                    ahead(nq + 1, 0)
                softmax_max(8 + 4 * layer + 3, 2, False)
                softmax_norm(base + 4, 1, False)
                softmax_max(8 + 4 * layer + 4, 3, False)
                if layer == 0:
                    ahead(nq + 1, 1)
                softmax_norm(base + 6, 2, False)
                softmax_norm(base + 8, 3, False)
                if layer == 0:
                    ahead(nq + 1, 2)
                    ahead(nq + 1, 3)
                else:
                    ahead(nq + 1, 0)
                for u in range(2):
                    i = (4 if layer == 0 else 10) + u + 1
                    dve.wait_ge(y_hi_ready, i)
                    dve.tensor_tensor(y_lo[:, KC + 2 * u:KC + 2 * u + 2, :],
                                      head[u][:].rearrange("p (h t) -> p h t", h=2),
                                      y_hi[:, KC + 2 * u:KC + 2 * u + 2, :].bitcast(F32), ALU.subtract
                                      ).then_inc(y_lo_ready, 1)

            def out_stage(name, layer, use):
                n = slab(name, (0, 0))
                ahead(n, 0)
                ahead(n, 1)
                if layer:
                    gated_d(1)
                ahead(n, 2)
                ahead(n, 3)
                if layer == 0:
                    gated_b(1)
                for q in range(4):
                    ahead(n + 1, q)
                ahead(n + 2, 0)
                mn_low(layer, use, range(0, 4))
                ahead(n + 2, 1)
                mn_low(layer, use, range(4, 8))
                ahead(n + 2, 2)
                ahead(n + 2, 3)
                ahead(n + 3, 0)
                add_turn(n + 2, 0)
                for q in range(1, 4):
                    ahead(n + 3, q)

            stage_a(0)
            stage_a(1)
            stage_b(0)
            stage_b(1)
            out_stage("OUT0", 0, 0)
            cross(0)
            no, n = slab("XA0", "o"), slab("XA1", "k")
            for q in range(4):
                ahead(no, q)
                if q == 1:
                    mn_low(1, 1, range(KC))
                if q == 2:
                    add_turn(no, 0, 0)
            add_turn(no, 1, 1)
            ahead(n, 0)
            norm_rows(3, x_sb, W[:, 0:2, :])
            for q in range(1, 4):
                ahead(n, q)
            xT_low(2, "od_norm", 0)

            def conv(g, u):
                cxp = wview(0, 2)[:, 0:4 * (S + 3)].rearrange("p (h t) -> p h t", h=4)
                xf = y_src(4 + g)
                dve.wait_ge(cx_ready, 2 * g + u + 1)
                dve.drain()
                for h in (2 * u, 2 * u + 1):
                    dve.tensor_scalar(xf[:, h, :], cxp[:, h, 0:S], param("od_conv_w", 4 * g + h),
                                      param("od_conv_b", 4 * g + h), ALU.mult, ALU.add)
                for j in range(1, 4):
                    dve.drain()
                    for h in (2 * u, 2 * u + 1):
                        last = dve.scalar_tensor_tensor(out=xf[:, h, :], in0=cxp[:, h, j:j + S],
                                                        scalar=param("od_conv_w", KC * j + 4 * g + h),
                                                        in1=xf[:, h, :], op0=ALU.mult, op1=ALU.add)
                last.then_inc(xf_ready, 1)

            def one_minus_a2(g):
                dve.wait_ge(a_squared, g + 1)
                dve.scalar_tensor_tensor(out=blocks(3), in0=y_src(4 + g), scalar=1.0, in1=blocks(3), op0=ALU.add,
                                         op1=ALU.mult).then_inc(one_minus, 1)
                dve.memset(blocks(5)[:, :, 0:1], 0.0)

            def gated_c(g):
                row = wview(2) if g == 0 else v_sb[:, :, :].rearrange("p t c -> p (t c)")
                dve.wait_ge(root_ready, g + 1)
                dve.tensor_tensor(wview(4), wview(4), wview(3), ALU.mult).then_inc(root_used, 1)
                dve.drain()
                dve.tensor_tensor_scan(row, wview(5), wview(4), 0.0, ALU.mult, ALU.add).then_inc(h_ready, 1)
                dve.drain()
                dve.wait_ge(z_ready, 8 + 2 * (g + 1))
                dve.tensor_tensor(row, row, zs[:].rearrange("p h t -> p (h t)"), ALU.mult).then_inc(y_ready, 1)

            def stage_c(g):
                cx, z = slab("C", "x", g), slab("C", "z", g)
                if g == 0:
                    cxp = wview(0, 2)[:, 0:4 * (S + 3)].rearrange("p (h t) -> p h t", h=4)
                    dve.memset(cxp[:, :, 0:3], 0.0)
                ahead(cx, 0)
                ahead(cx, 1)
                ahead(cx, 2)
                conv(g, 0)
                ahead(cx, 3)
                ahead(z, 0)
                conv(g, 1)
                ahead(z, 1)
                if g:
                    one_minus_a2(0)
                ahead(z, 2)
                ahead(z, 3)
                if g:
                    gated_c(0)

            def rope_full(n, u, w, done):
                filled(dve, n, u)
                src = bank(n, u)[:].rearrange("p (h t) -> p h t", h=2)
                dst = blocks(w)[:, 2 * u:2 * u + 2, :]
                tmp = rope_tmp[:, 2 * u:2 * u + 2, :]
                dve.drain()
                for a, b in ((0, 64), (64, 0)):
                    dve.tensor_tensor(tmp[a:a + 64], src[b:b + 64], trig[b:b + 64, 1:2, :].broadcast_to([64, 2, S]),
                                      ALU.mult)
                dve.tensor_tensor(dst, src, trig[:, 0:1, :].broadcast_to([P, 2, S]), ALU.mult)
                dve.drain().then_inc(free_of(n, u), 1)
                dve.tensor_tensor(dst, dst, tmp, ALU.add).then_inc(done, 1)

            def gated_d(g):
                dve.wait_ge(o_rstd, 3 + g)
                if g:
                    dve.wait_ge(y_lo_ready, 9)
                for h in range(4):
                    dve.scalar_tensor_tensor(out=blocks(2)[:, h, :], in0=head[2 + h // 2][:, S * (h % 2):S * (h % 2) + S],
                                             scalar=param("od_ret_gain", 4 * g + h), in1=blocks(4)[:, h, :],
                                             op0=ALU.mult, op1=ALU.mult)
                dve.drain()
                dve.wait_ge(z_ready, 12 + 2 * (g + 1))
                for h in range(4):
                    last = dve.scalar_tensor_tensor(out=blocks(2)[:, h, :], in0=blocks(2)[:, h, :],
                                                    scalar=param("od_ret_bias", 4 * g + h), in1=zs[:, h, :],
                                                    op0=ALU.add, op1=ALU.mult)
                last.then_inc(y_ready, 1)

            def decayed(g, hs):
                for h in hs:
                    i = 4 * g + h
                    dve.wait_ge(dmask_ready, i + 1)
                    dve.wait_ge(att_psum, 4 + i + 1)
                    dve.tensor_tensor(am[:, h, :], head[h][:, 0:384], dmask[:, h, :], ALU.mult).then_inc(att_ready, 1)

            def stage_d(g):
                q, k, v, z = (slab("D", c, g) for c in "qkvz")
                ahead(q, 0)
                ahead(q, 1)
                if g:
                    gated_d(0)
                ahead(q, 2)
                rope_full(q, 0, 0, q_ready)
                ahead(q, 3)
                ahead(k, 0)
                rope_full(q, 1, 0, q_ready)
                ahead(k, 1)
                if g == 0:
                    one_minus_a2(1)
                ahead(k, 2)
                rope_full(k, 0, 1, k_ready)
                ahead(k, 3)
                ahead(v, 0)
                rope_full(k, 1, 1, k_ready)
                ahead(v, 1)
                if g == 0:
                    gated_c(1)
                ahead(v, 2)
                ahead(v, 3)
                decayed(g, (0, 1))
                ahead(z, 0)
                decayed(g, (2, 3))
                for j in range(1, 4):
                    ahead(z, j)

            def times_gain(c):
                for t in (1, 0):
                    last = dve.tensor_tensor(W[:, 2 + t, 512 * c:512 * c + 512], x_sb[:, t, 512 * c:512 * c + 512],
                                             fgain[:, 512 * c:512 * c + 512], ALU.mult)
                    if t:
                        last.then_inc(gained, 1)

            stage_c(0)
            stage_c(1)
            stage_d(0)
            stage_d(1)
            out_stage("OUT1", 1, 2)
            cross(1)
            add_turn(slab("XA1", "o"), 0, 0)
            dve.wait_ge(fgain_landed, 16)
            times_gain(0)
            add_turn(slab("XA1", "o"), 1, 1)
            times_gain(1)
            rstd(5)
            for c in range(2):
                part = slice(512 * c, 512 * c + 512)
                dve.tensor_scalar(x_sb[:, 0, part], W[:, 2, part], st[:, 6:7], None, ALU.mult).then_inc(fin_ready, 1)

        @block.tensor
        def _(pe):
            def split_ready(n, q):
                pe.wait_ge(hi_ready, 4 * n + q + 1)
                pe.wait_ge(lo_ready, 4 * n + q + 1)

            def take_bank(n, u, half=0):
                before = (TURN[n] + half) // 2
                if before >= 1:
                    pe.wait_ge(free_of(n, u, half), before)

            def quarter_f(n, q, x_hi=xT_hi, x_lo=xT_lo, norm=None, four_banks=False):
                if four_banks:
                    u, half, col = q % 2, q // 2, 0
                    take_bank(n, u, half)
                else:
                    u, half, col = q // 2, 0, S * (q % 2)
                    if q % 2 == 0:
                        take_bank(n, u)
                split_ready(n, q)
                dst = bank(n, u, half)[:, col:col + S]
                wh, wl = ring_quarter(w_hi, n, q), ring_quarter(w_lo, n, q)
                for k in range(KC):
                    if norm is not None:
                        pe.wait_ge(xT_lo_ready, KC * norm + k + 1)
                    pe.matmul(dst, wh[:, k, :], x_hi[:, k, :], start=(k == 0), stop=False)
                    pe.matmul(dst, wh[:, k, :], x_lo[:, k, :], start=False, stop=False)
                    last = pe.matmul(dst, wl[:, k, :], x_hi[:, k, :], start=False, stop=(k == KC - 1))
                last.then_inc(quarter_used, 1)

            def quarter_t(n, q, x_hi, x_lo, k0, half=0, start=True, stop=True):
                first = start and (q % 2 == 0 if SLABS[n][2] == "W" else q == 0)
                final = stop and (q % 2 == 1 if SLABS[n][2] == "W" else q == 3)
                if first:
                    for t in range(T):
                        take_bank(n, t, half)
                split_ready(n, q)
                wh, wl = ring_quarter(w_hi, n, q), ring_quarter(w_lo, n, q)
                for t in range(T):
                    dst = bank(n, t, half)[:]
                    tok = slice(P * t, P * t + P)
                    for k in range(2):
                        pe.matmul(dst, x_hi[:, k0 + k, tok], wh[:, k, :], start=first and k == 0, stop=False)
                        pe.matmul(dst, x_lo[:, k0 + k, tok], wh[:, k, :], start=False, stop=False)
                        last = pe.matmul(dst, x_hi[:, k0 + k, tok], wl[:, k, :], start=False, stop=final and k == 1)
                    if t == 0 and n == NSLAB - 1 and q == 3:
                        last.then_inc(first_tile_filled, 1)
                last.then_inc(quarter_used, 1)

            def slab_f(n, qs=range(4), x=(xT_hi, xT_lo), norm=None):
                for q in qs:
                    quarter_f(n, q, x[0], x[1], norm=norm if q == 0 else None)

            def slab_t(n, qs=range(4), x=(xT_hi, xT_lo), k0=0, start=True, stop=True):
                for q in qs:
                    quarter_t(n, q, x[0], x[1], k0 + 2 * q, start=start, stop=stop)

            def turn_rows(src, norm, ks=range(KC)):
                for k in ks:
                    if k % 4 == 0:
                        pe.wait_ge(normed, 2 * norm + k // 4 + 1)
                    for t in range(T):
                        last = pe.transpose(head[k // 2][:, S * (k % 2) + P * t:S * (k % 2) + P * t + P],
                                            src[:, t, P * k:P * k + P], ident[:])
                    if k % 2:
                        last.then_inc(turned, 1)

            pe.wait_ge(masks_ready, 1)
            turn_rows(W[:, 0:2, :], 0, range(6))
            pe.wait_ge(prm_landed, 16 * len(PARAM_ROWS))
            pe.transpose(proj[0][:, 0:P], prm_rows[:, 0, :], ident[:])
            pe.transpose(proj[0][:, P:N_ROWS], prm_rows[0:N_ROWS - P, 1, :], ident[0:N_ROWS - P, 0:N_ROWS - P]
                         ).then_inc(prm_turned, 1)
            turn_rows(W[:, 0:2, :], 0, range(6, KC))
            pe.wait_ge(prm_ready, 1)

            def own_states(g, h0):
                for h in (h0, h0 + 1):
                    for c in range(NCH - 1):
                        t, j = divmod(c, 4)
                        r = slice(HGRN_CHUNK * j, HGRN_CHUNK * j + HGRN_CHUNK)
                        last = pe.matmul(head[j][:, P * (2 * (h % 2) + t):P * (2 * (h % 2) + t) + P],
                                         kend_rows[r, t, h, :], v_sb[r, t, P * h:P * h + P], start=True, stop=True)
                last.then_inc(u_psum, 1)

            def out_a(g):
                pe.wait_ge(state_ready, 4 * g + 4)
                for h in range(4):
                    dst = head[h // 2][:, S * (h % 2):S * (h % 2) + S]
                    for t in range(T):
                        pe.matmul(dst[:, P * t:P * t + P], v_sb[:, t, P * h:P * h + P], att[:, h, P * t:P * t + P],
                                  start=(t == 0), stop=False, skip_group_check=True)
                    for c in range(1, NCH):
                        last = pe.matmul(dst[:, HGRN_CHUNK * c:HGRN_CHUNK * c + HGRN_CHUNK], states[:, h, c - 1, :],
                                         W[:, 4, S * h + HGRN_CHUNK * c:S * h + HGRN_CHUNK * c + HGRN_CHUNK],
                                         start=False, stop=(c == NCH - 1), skip_group_check=True)
                    if h % 2:
                        last.then_inc(o_psum, 1)

            def mean_square_a(g):
                for u in range(2):
                    pe.wait_ge(o_square, 2 * g + u + 1)
                    pe.matmul(head[2 + u][:], avg[:], W[:, 5, 512 * u:512 * u + 512], start=True, stop=True
                              ).then_inc(ms_psum, 1)

            def stage_a(g):
                f, q, i, z = (slab("A", c, g) for c in "fqiz")
                slab_f(f, [0, 1, 2], norm=0 if g == 0 else None)
                if g:
                    out_a(0)
                slab_f(f, [3])
                if g:
                    mean_square_a(0)
                slab_f(q)
                slab_t(i)
                pe.wait_ge(kinv_ready, g + 1)
                pe.wait_ge(qdec_ready, 2 * g + 2)
                if g:
                    pe.wait_ge(y_ready, g)
                for h in range(4):
                    for t in range(T):
                        c = S * h + P * t
                        last = pe.matmul(head[h // 2][:, S * (h % 2) + P * t:S * (h % 2) + P * t + P],
                                         W[:, 0, c:c + P], W[:, 4, c:c + P], start=True, stop=True)
                    if h % 2:
                        last.then_inc(att_psum, 1)
                pe.wait_ge(kend_ready, g + 1)
                for t in range(T):
                    for h in range(4):
                        last = pe.transpose(head[2 + t][:, P * h:P * h + P], W[:, 1, S * h + P * t:S * h + P * t + P],
                                            ident[:])
                    last.then_inc(kend_turned, 1)
                slab_f(z, [0, 1])
                pe.wait_ge(att_ready, 4 * g + 4)
                pe.wait_ge(kend_rows_ready, 2 * g + 2)
                pe.wait_ge(v_ready, 2 * g + 2)
                own_states(g, 0)
                slab_f(z, [2, 3])
                pe.wait_ge(state_ready, 4 * g + 2)
                own_states(g, 2)

            def values_out(h, spans):
                dst = head[h // 2][:, S * (h % 2):S * (h % 2) + S]
                for j, (t, a, w, src) in enumerate(spans):
                    last = pe.matmul(dst[:, a:a + w], v_sb[:, t, P * h:P * h + P], src, start=(j == 0),
                                     stop=(j == len(spans) - 1), skip_group_check=True)
                return last

            def turn_probs_b(g):
                for h in range(4):
                    pe.wait_ge(probs_norm, 4 * g + h + 1)
                    for c in range(3):
                        last = pe.transpose(head[h][:, P * c:P * c + P],
                                            wview(2, 2)[:, 384 * h + P * c:384 * h + P * c + P], ident[:])
                    last.then_inc(probs_turned, 1)

            def out_b(g):
                pe.wait_ge(v_ready, 4 + 2 * g + 2)
                pe.wait_ge(probsT_ready, 4 * g + 4)
                for h in range(4):
                    pt = wview(4, 2)[:, 384 * h:384 * h + 384]
                    last = values_out(h, [(0, 0, S, pt[:, 0:S]), (1, P, P, pt[:, S:3 * P])])
                    if h % 2:
                        last.then_inc(o_psum, 1)

            def stage_b(g):
                q, k, v, z = (slab("B", c, g) for c in "qkvz")
                if g == 0:
                    slab_f(q, [0, 1, 2])
                    out_a(1)
                    slab_f(q, [3])
                    mean_square_a(1)
                    slab_f(k)
                    slab_t(v)
                else:
                    slab_f(q, [0, 1])
                    turn_probs_b(0)
                    slab_f(q, [2])
                    out_b(0)
                    slab_f(q, [3])
                    slab_f(k)
                    slab_t(v, [0])
                    pe.wait_ge(y_ready, 3)
                    turn_rows(mem_rows, 1)
                    slab_t(v, [1, 2, 3])
                slab_f(z, [0])
                if g:
                    pe.wait_ge(memT_ready, 4)
                pe.wait_ge(q_ready, g + 1)
                pe.wait_ge(k_ready, g + 1)
                pe.wait_ge(y_ready, 2 + g)
                for h in range(4):
                    pe.matmul(head[h][:, 0:P], W[:, 0, S * h:S * h + P], W[:, 1, S * h:S * h + P],
                              start=True, stop=True)
                    pe.matmul(head[h][:, P:3 * P], W[:, 0, S * h + P:S * h + S], W[:, 1, S * h:S * h + S],
                              start=True, stop=True).then_inc(scores, 1)
                slab_f(z, [1, 2, 3])

            def out_proj(name, layer):
                n = slab(name, (0, 0))
                done = 4 if layer == 0 else 10
                pe.wait_ge(y_lo_ready, done - 2)
                slab_t(n, [0], x=(y_hi, y_lo), stop=False)
                if layer:
                    mean_square_d(1)
                slab_t(n, [1], x=(y_hi, y_lo), stop=False)
                if layer == 0:
                    turn_probs_b(1)
                slab_t(n, [2], x=(y_hi, y_lo), stop=False)
                if layer == 0:
                    out_b(1)
                slab_t(n, [3], x=(y_hi, y_lo), stop=False)
                slab_t(n + 1, x=(y_hi, y_lo), stop=False)
                pe.wait_ge(y_lo_ready, done)
                slab_t(n + 2, x=(y_hi, y_lo), k0=KC, start=False)
                slab_t(n + 3, x=(y_hi, y_lo), k0=KC, start=False)

            def cross(layer):
                X = f"XA{layer}"
                nk, nq, nv, no = (slab(X, c) for c in "kqvo")
                pe.wait_ge(mn_lo_ready, KC * (2 * layer + 1))
                if layer == 0:
                    slab_f(nk, x=(y_hi, y_lo))
                else:
                    slab_t(nv, x=(y_hi, y_lo))
                i = 1 + 2 * layer
                turn_rows(W[:, 0:2, :], 2 + 2 * layer)

                def score(h):
                    pe.wait_ge(q_rows, 4 + 4 * layer + h + 1)
                    if h == 0:
                        pe.wait_ge(k_rows, 6 + 2 * layer)
                    for t in range(T):
                        last = pe.matmul(head[h][:, S * t:S * t + S], W[:, 0, S * h + P * t:S * h + P * t + P],
                                         kx[:, h, :], start=True, stop=True)
                    last.then_inc(scores, 1)

                def turn_probs(h):
                    pe.wait_ge(probs_norm, 8 + 4 * layer + h + 1)
                    for t in range(T):
                        for kt in range(T):
                            last = pe.transpose(head[h][:, S * kt + P * t:S * kt + P * t + P],
                                                wview(2, 2)[:, 512 * h + S * t + P * kt:512 * h + S * t + P * kt + P],
                                                ident[:])
                    last.then_inc(probs_turned, 1)

                for q in range(4):
                    quarter_f(nq, q, norm=i if q == 0 else None, four_banks=True)
                    if q >= 1:
                        score(q - 1)
                if layer == 0:
                    slab_t(nv, [0], x=(y_hi, y_lo))
                score(3)
                if layer == 0:
                    slab_t(nv, [1, 2], x=(y_hi, y_lo))
                for h in range(2):
                    turn_probs(h)
                if layer == 0:
                    slab_t(nv, [3], x=(y_hi, y_lo))
                for h in range(2, 4):
                    turn_probs(h)
                pe.wait_ge(v_ready, (10 if layer == 0 else 16))
                for h in range(4):
                    pe.wait_ge(probsT_ready, 8 + 4 * layer + max(h + 1, 2))
                    pt = wview(4, 2)[:, 512 * h:512 * h + 512]
                    last = values_out(h, [(0, 0, S, pt[:, 0:S]), (1, 0, S, pt[:, S:2 * S])])
                    if h % 2:
                        last.then_inc(o_psum, 1)
                for q in range(4):
                    if q < 2:
                        pe.wait_ge(y_lo_ready, (5 if layer == 0 else 11) + q)
                    quarter_t(no, q, y_hi, y_lo, KC + 2 * (q % 2), half=q // 2)

            stage_a(0)
            stage_a(1)
            stage_b(0)
            stage_b(1)
            out_proj("OUT0", 0)
            cross(0)
            pe.wait_ge(mn_lo_ready, 2 * KC)
            slab_f(slab("XA1", "k"), x=(y_hi, y_lo))
            turn_rows(W[:, 0:2, :], 3)

            def gates(g):
                pe.wait_ge(rg_landed[g], 32)
                for m in range(2):
                    for h in range(4):
                        if m == 0 and h % 2 == 0:
                            pe.wait_ge(xf_ready, 2 * g + h // 2 + 1)
                        last = pe.matmul(head[2 * m + h // 2][:, S * (h % 2):S * (h % 2) + S], rg_w[:, 2 * g + m, h, :],
                                         y_src(4 + g)[:, h, :], start=True, stop=True)
                        if h % 2:
                            last.then_inc(gates_psum, 1)

            def stage_c(g):
                cx, z = slab("C", "x", g), slab("C", "z", g)
                slab_f(cx, norm=2 if g == 0 else None)
                slab_f(z)
                if g:
                    pe.wait_ge(igate_ready, g)
                gates(g)

            def mean_square_d(g):
                for u in range(2):
                    pe.wait_ge(o_square, 4 + 2 * g + u + 1)
                    pe.matmul(head[u][:], avg[:], W[:, 5, 512 * u:512 * u + 512], start=True, stop=True
                              ).then_inc(ms_psum, 1)

            def stage_d(g):
                q, k, v, z = (slab("D", c, g) for c in "qkvz")
                slab_f(q, [0])
                if g:
                    mean_square_d(0)
                slab_f(q, [1, 2, 3])
                slab_f(k)
                slab_t(v)
                pe.wait_ge(q_ready, 2 + 2 * g + 2)
                pe.wait_ge(k_ready, 2 + 2 * g + 2)
                pe.wait_ge(y_ready, 5 if g == 0 else 7)
                pe.wait_ge(igate_ready, 2)
                for h in range(4):
                    pe.matmul(head[h][:, 0:S], W[:, 1, S * h:S * h + P], W[:, 0, S * h:S * h + S],
                              start=True, stop=True)
                    pe.matmul(head[h][:, S:3 * P], W[:, 1, S * h + P:S * h + S], W[:, 0, S * h + P:S * h + S],
                              start=True, stop=True).then_inc(att_psum, 1)
                slab_f(z, [0, 1])
                pe.wait_ge(v_ready, 10 + 2 * g + 2)
                pe.wait_ge(att_ready, 8 + 4 * g + 4)
                for h in range(4):
                    last = values_out(h, [(0, 0, S, am[:, h, 0:S]), (1, P, P, am[:, h, S:3 * P])])
                    if h % 2:
                        last.then_inc(o_psum, 1)
                slab_f(z, [2])
                for u in range(2):
                    pe.wait_ge(o_copied, 2 * g + u + 1)
                    pe.matmul(head[2 + u][:], center[:], W[:, 4, 512 * u:512 * u + 512], start=True, stop=True
                              ).then_inc(cen_psum, 1)
                slab_f(z, [3])

            stage_c(0)
            stage_c(1)
            stage_d(0)
            stage_d(1)
            out_proj("OUT1", 1)
            cross(1)


def shape_constants():
    c = np.zeros((P, N_CONST), np.float32)
    p = np.arange(P)
    ret = np.float32(10000.0) ** (-(np.arange(64, dtype=np.float32)) / np.float32(64))
    moba = np.float32(500000.0) ** (-(np.arange(16, dtype=np.float32)) / np.float32(16))
    c[:, C_INV_RET] = ret[p % 64]
    c[:32, C_INV_MOBA] = moba[p[:32] % 16]
    c[:, C_SIGN_RET] = np.where(p < 64, 1.0, -1.0)
    c[:, C_SIGN_MOBA] = np.where(p < 16, -1.0, 1.0)
    c[:, C_LOG_G:C_LOG_G + 8] = np.log1p(-2.0 ** (-5.0 - np.arange(8.0)))[None, :]
    return c


_INS = ['x', 'mem', 'positions', 'hgrn_lb_logits', 'ev_norm', 'ev_w_in', 'ev_hgrn_gain', 'ev_w_out', 'od_norm',
        'od_w_in', 'od_conv_w', 'od_conv_b', 'od_rg_wa', 'od_rg_ba', 'od_rg_wx', 'od_rg_bx', 'od_rg_lambda',
        'od_ret_gain', 'od_ret_bias', 'od_w_out', 'xa_norm', 'xa_mem_norm', 'xa_wq', 'xa_wkv', 'xa_wo', 'final_norm']


def kernel(**inputs):
    import numpy as _np
    import concourse.bacc as _bacc
    from concourse import mybir as _mybir
    from concourse.bass_utils import run_bass_kernel_spmd as _run

    nc = _bacc.Bacc("TRN2", target_bir_lowering=False, num_devices=1)
    arrays, aps = {}, {}
    given = {name: _np.ascontiguousarray(inputs[name]) for name in _INS}
    given["shape_constants"] = shape_constants()
    for name, a in given.items():
        arrays[f"in_{name}_dram"] = a
        aps[name] = nc.dram_tensor(f"in_{name}_dram", a.shape, _mybir.dt.from_np(a.dtype), kind="ExternalInput").ap()
    out = nc.dram_tensor("out_0_dram", (1, S, D), F32, kind="ExternalOutput").ap()
    hybrid_trunk(nc, aps, out)
    r = _run(nc, [arrays], core_ids=[0])
    return r.results[0]["out_0_dram"]
```
